# Optimizing a Trainium2 kernel written in Bass

```python
import math
import jax, jax.numpy as jnp
from jax import lax
import numpy as np

D_MODEL = 1024
BATCH = 1
SEQ = 1024
DEPTH = 1
DEC_BATCH = 8
DEC_SEQ = 4
PAST_LEN = 2048
PAGE_SIZE = 128

H_A = 8
G_A = 2
R_A = H_A // G_A
HD_A = 64
W_A = H_A * HD_A
N_KV_A = 6
N_KV_SEL = 4
CMP_BLOCK = 32
CMP_STRIDE = 16
SEL_BLOCK = 64
N_SEL = 16
WINDOW = 512
FORCE_SCORE = 1e4
H_B = 4
NOPE = 128
ROPE_DIM = 64
V_HEAD = 128
Q_LORA = 256
KV_LORA = 128
W_B = H_B * V_HEAD
ROPE_BASE = 10000.0
N_BUCKETS = 32
MAX_DIST = 128
QBLK = 128
EPS = 1e-6
NEG_BIG = -1e30
IN_SIZES = (W_A, N_KV_A * G_A * HD_A, 3 * H_A, W_A, Q_LORA, KV_LORA, ROPE_DIM, W_B)
N_IN = W_A + N_KV_A * G_A * HD_A + 3 * H_A + W_A + Q_LORA + KV_LORA + ROPE_DIM + W_B

kernel_name = 'hymba_nsa_mla_decode_step'

def rmsnorm(x, g):
    xf = x.astype(jnp.float32)
    y = xf * lax.rsqrt(jnp.mean(xf * xf, axis=-1, keepdims=True) + EPS)
    return (y * g.astype(jnp.float32)).astype(x.dtype)

def masked_softmax(s, valid):
    s = jnp.where(valid, s.astype(jnp.float32), NEG_BIG)
    return jnp.where(valid, jax.nn.softmax(s, axis=-1), 0.0)

def rel_bucket(dist):
    n = jnp.maximum(dist, 0)
    max_exact = N_BUCKETS // 2
    nf = jnp.maximum(n, 1).astype(jnp.float32)
    large = max_exact + (jnp.log(nf / max_exact) / math.log(MAX_DIST / max_exact)
                         * (N_BUCKETS - max_exact)).astype(jnp.int32)
    large = jnp.minimum(large, N_BUCKETS - 1)
    return jnp.where(n < max_exact, n, large)

def apply_rope(x, pos):
    half = x.shape[-1] // 2
    inv = ROPE_BASE ** (-jnp.arange(half, dtype=jnp.float32) / half)
    ang = pos.astype(jnp.float32)[:, None] * inv[None, :]
    cos = jnp.cos(ang)[None, :, None, :]
    sin = jnp.sin(ang)[None, :, None, :]
    xf = x.astype(jnp.float32)
    x1, x2 = xf[..., :half], xf[..., half:]
    return jnp.concatenate([x1 * cos - x2 * sin, x1 * sin + x2 * cos], axis=-1).astype(x.dtype)

def project(x, c, q_pos, w_ada, b_ada, g_norm, w_in, g_q_lat, w_uq, g_kv_lat, w_uk):
    B, T = x.shape[0], x.shape[1]
    mod = c @ w_ada + b_ada
    shift, scale, gate = jnp.split(mod, 3, axis=-1)
    h = rmsnorm(x, g_norm) * (1.0 + scale[:, None, :]) + shift[:, None, :]
    u = h @ w_in
    cuts = []
    acc = 0
    for s in IN_SIZES[:-1]:
        acc += s
        cuts.append(acc)
    q_a, kv_a, g_logit, z_a, cq, ckv, kr, z_b = jnp.split(u, cuts, axis=-1)
    q_a = q_a.reshape(B, T, G_A, R_A, HD_A)
    kv_a = kv_a.reshape(B, T, N_KV_A, G_A, HD_A)
    gates = jax.nn.sigmoid(g_logit.reshape(B, T, G_A, R_A, 3))
    q_b = jnp.einsum('btq,qhe->bthe', rmsnorm(cq, g_q_lat), w_uq)
    q_rope = apply_rope(q_b[..., NOPE:], q_pos)
    q_lat = jnp.einsum('bthn,rhn->bthr', q_b[..., :NOPE], w_uk)
    k_rope = apply_rope(kr[:, :, None, :], q_pos)[:, :, 0, :]
    mla_row = jnp.concatenate([rmsnorm(ckv, g_kv_lat), k_rope], axis=-1)
    return gate, q_a, kv_a, gates, z_a, q_lat, q_rope, mla_row, z_b

def compress(k, w, pe):
    B, L = k.shape[0], k.shape[1]
    n_chunks = L // CMP_STRIDE
    ch = k[:, :n_chunks * CMP_STRIDE].reshape(B, n_chunks, CMP_STRIDE, G_A, HD_A)
    blk = jnp.concatenate([ch[:, :-1], ch[:, 1:]], axis=2) + pe[None, None, :, None, :]
    return jnp.einsum('bnlgd,lde->bnge', blk, w)

def cmp_block_ends(n_cmp):
    return jnp.arange(n_cmp, dtype=jnp.int32) * CMP_STRIDE + CMP_BLOCK - 1

def sel_blocks(k):
    B, L = k.shape[0], k.shape[1]
    pad = (-L) % SEL_BLOCK
    kp = jnp.pad(k, ((0, 0), (0, pad), (0, 0), (0, 0)))
    return kp.reshape(B, (L + pad) // SEL_BLOCK, SEL_BLOCK, G_A, HD_A)

def overlap_matrix(n_cmp, n_sel):
    cs = jnp.arange(n_cmp)[:, None] * CMP_STRIDE
    ss = jnp.arange(n_sel)[None, :] * SEL_BLOCK
    ov = jnp.minimum(cs + CMP_BLOCK, ss + SEL_BLOCK) - jnp.maximum(cs, ss)
    return jnp.maximum(ov, 0).astype(jnp.float32) / CMP_BLOCK

def nsa_cmp_sel(q, q_pos, kc, vc, c_end, ks_b, vs_b, m_ov, rel_bias):
    scale = HD_A ** -0.5
    table = rel_bias.reshape(N_BUCKETS, G_A, R_A)
    s = jnp.einsum('btgrd,bngd->btgrn', q, kc).astype(jnp.float32) * scale
    dist = q_pos[:, None] - c_end[None, :]
    bias = table[rel_bucket(dist)].transpose(0, 2, 3, 1)[None]
    p_c = masked_softmax(s + bias, (dist >= 0)[None, :, None, None, :])
    o_cmp = jnp.einsum('btgrn,bngd->btgrd', p_c.astype(vc.dtype), vc)
    imp = jnp.einsum('btgrn,ns->btgs', p_c, m_ov)
    ns = ks_b.shape[1]
    jj = jnp.arange(ns)[None, :]
    cc = (q_pos // SEL_BLOCK)[:, None]
    forced = (jj == 0) | (jj == cc) | (jj == cc - 1)
    score = jnp.where(forced[None, :, None, :], FORCE_SCORE,
                      jnp.where((jj <= cc)[None, :, None, :], imp, -jnp.inf))
    _, idx = lax.top_k(score, min(N_SEL, ns))
    idx_t = idx.transpose(0, 2, 1, 3)
    gather = jax.vmap(jax.vmap(lambda kb, ix: kb[ix]))
    gk = gather(ks_b.transpose(0, 3, 1, 2, 4), idx_t)
    gv = gather(vs_b.transpose(0, 3, 1, 2, 4), idx_t)
    tok = idx_t[..., None] * SEL_BLOCK + jnp.arange(SEL_BLOCK)
    dist_s = q_pos[None, None, :, None, None] - tok
    bias_s = table[rel_bucket(dist_s), jnp.arange(G_A)[None, :, None, None, None]]
    s2 = jnp.einsum('btgrd,bgtksd->bgtrks', q, gk).astype(jnp.float32) * scale
    s2 = s2 + bias_s.transpose(0, 1, 2, 5, 3, 4)
    B, G, T, R, K, SB = s2.shape
    valid = jnp.broadcast_to((dist_s >= 0)[:, :, :, None], s2.shape)
    p_s = masked_softmax(s2.reshape(B, G, T, R, K * SB), valid.reshape(B, G, T, R, K * SB))
    o_sel = jnp.einsum('bgtrks,bgtksd->btgrd', p_s.reshape(s2.shape).astype(gv.dtype), gv)
    return o_cmp, o_sel

def window_attend(q, q_pos, k, v, k_pos, rel_bias):
    scale = HD_A ** -0.5
    s = jnp.einsum('bntgrd,bnsgd->bngrts', q, k).astype(jnp.float32) * scale
    dist = q_pos[:, :, None] - k_pos[:, None, :]
    n, t, sk = dist.shape
    bias = rel_bias[rel_bucket(dist)].reshape(n, t, sk, G_A, R_A).transpose(0, 3, 4, 1, 2)
    valid = (dist >= 0) & (dist < WINDOW) & (k_pos[:, None, :] >= 0)
    p = masked_softmax(s + bias[None], valid[None, :, None, None])
    return jnp.einsum('bngrts,bnsgd->bntgrd', p.astype(v.dtype), v)

def mla_attend(q_lat, q_rope, ckv, k_rope, q_pos, k_pos):
    scale = (NOPE + ROPE_DIM) ** -0.5
    s = (jnp.einsum('bthr,blr->bhtl', q_lat, ckv)
         + jnp.einsum('bthe,ble->bhtl', q_rope, k_rope)).astype(jnp.float32) * scale
    valid = (k_pos[None, :] <= q_pos[:, None])[None, None]
    p = masked_softmax(s, valid)
    return jnp.einsum('bhtl,blr->bthr', p.astype(ckv.dtype), ckv)

def map_query_blocks(fn, qs, q_pos):
    T = q_pos.shape[0]
    nb = T // QBLK
    def to_blocks(a):
        return jnp.moveaxis(a.reshape(a.shape[0], nb, QBLK, *a.shape[2:]), 1, 0)
    def from_blocks(a):
        a = jnp.moveaxis(a, 0, 1)
        return a.reshape(a.shape[0], T, *a.shape[3:])
    outs = lax.map(lambda a: fn(*a[0], a[1]),
                   (tuple(to_blocks(q) for q in qs), q_pos.reshape(nb, QBLK)))
    return jax.tree_util.tree_map(from_blocks, outs)

def merge_out(x, gate, gates, o_cmp, o_sel, o_win, z_a, o_lat, z_b, w_uv, w_out):
    B, T = x.shape[0], x.shape[1]
    o_a = gates[..., 0:1] * o_cmp + gates[..., 1:2] * o_sel + gates[..., 2:3] * o_win
    y_a = o_a.reshape(B, T, W_A) * jax.nn.silu(z_a)
    y_b = jnp.einsum('bthr,rhv->bthv', o_lat, w_uv).reshape(B, T, W_B) * jax.nn.silu(z_b)
    out = jnp.concatenate([y_a, y_b], axis=-1) @ w_out
    return x + gate[:, None, :] * out

def prompt_layer(x, c, lw, cw, rel_bias, w_uv, w_out):
    B, T = x.shape[0], x.shape[1]
    pos = jnp.arange(T, dtype=jnp.int32)
    gate, q_a, kv_a, gates, z_a, q_lat, q_rope, mla_row, z_b = project(x, c, pos, *lw)
    w_ck, w_cv, pe_k, pe_v = cw
    kc = compress(kv_a[:, :, 0], w_ck, pe_k)
    vc = compress(kv_a[:, :, 1], w_cv, pe_v)
    c_end = cmp_block_ends(kc.shape[1])
    ks_b = sel_blocks(kv_a[:, :, 2])
    vs_b = sel_blocks(kv_a[:, :, 3])
    m_ov = overlap_matrix(kc.shape[1], ks_b.shape[1])
    o_cmp, o_sel = map_query_blocks(
        lambda q, p: nsa_cmp_sel(q, p, kc, vc, c_end, ks_b, vs_b, m_ov, rel_bias), (q_a,), pos)
    nb = T // QBLK
    nw = WINDOW // QBLK
    def band(a):
        ap = jnp.pad(a, ((0, 0), (WINDOW, 0), (0, 0), (0, 0))).reshape(B, nb + nw, QBLK, G_A, HD_A)
        return jnp.concatenate([ap[:, i:i + nb] for i in range(nw + 1)], axis=2)
    k_pos = jnp.arange(nb, dtype=jnp.int32)[:, None] * QBLK - WINDOW + jnp.arange((nw + 1) * QBLK, dtype=jnp.int32)[None, :]
    o_win = window_attend(q_a.reshape(B, nb, QBLK, G_A, R_A, HD_A), pos.reshape(nb, QBLK),
                          band(kv_a[:, :, 4]), band(kv_a[:, :, 5]), k_pos, rel_bias).reshape(B, T, G_A, R_A, HD_A)
    ckv, k_rope = mla_row[..., :KV_LORA], mla_row[..., KV_LORA:]
    o_lat = map_query_blocks(lambda ql, qr, p: mla_attend(ql, qr, ckv, k_rope, p, pos), (q_lat, q_rope), pos)
    x = merge_out(x, gate, gates, o_cmp, o_sel, o_win, z_a, o_lat, z_b, w_uv, w_out)
    new_win = kv_a[:, T - min(WINDOW, T):, 4:6]
    return x, kv_a[:, :, :N_KV_SEL], mla_row, new_win

def sample_layer(x, c, cache_nsa_l, cache_mla_l, win_l, page_table, lw, cw, rel_bias, w_uv, w_out):
    Bd, T = x.shape[0], x.shape[1]
    pos = PAST_LEN + jnp.arange(T, dtype=jnp.int32)
    gate, q_a, kv_a, gates, z_a, q_lat, q_rope, mla_row, z_b = project(x, c, pos, *lw)
    w_ck, w_cv, pe_k, pe_v = cw
    past_nsa = cache_nsa_l[page_table].reshape(Bd, PAST_LEN, N_KV_SEL, G_A, HD_A)
    full = jnp.concatenate([past_nsa, kv_a[:, :, :N_KV_SEL]], axis=1)
    kc = compress(full[:, :, 0], w_ck, pe_k)
    vc = compress(full[:, :, 1], w_cv, pe_v)
    c_end = cmp_block_ends(kc.shape[1])
    ks_b = sel_blocks(full[:, :, 2])
    vs_b = sel_blocks(full[:, :, 3])
    m_ov = overlap_matrix(kc.shape[1], ks_b.shape[1])
    o_cmp, o_sel = nsa_cmp_sel(q_a, pos, kc, vc, c_end, ks_b, vs_b, m_ov, rel_bias)
    wb = win_l.shape[1]
    kvw = jnp.concatenate([win_l, kv_a[:, :, 4:6]], axis=1)
    k_pos = (PAST_LEN - wb + jnp.arange(wb + T, dtype=jnp.int32))[None]
    o_win = window_attend(q_a[:, None], pos[None], kvw[:, None, :, 0], kvw[:, None, :, 1], k_pos, rel_bias)[:, 0]
    past_mla = cache_mla_l[page_table].reshape(Bd, PAST_LEN, KV_LORA + ROPE_DIM)
    full_mla = jnp.concatenate([past_mla, mla_row], axis=1)
    o_lat = mla_attend(q_lat, q_rope, full_mla[..., :KV_LORA], full_mla[..., KV_LORA:], pos,
                       jnp.arange(PAST_LEN + T, dtype=jnp.int32))
    x = merge_out(x, gate, gates, o_cmp, o_sel, o_win, z_a, o_lat, z_b, w_uv, w_out)
    return x, kv_a[:, :, :N_KV_SEL], mla_row, kvw[:, T:]

def setup_inputs(seed: int = 0) -> dict:
    key = jax.random.key(seed)
    ks = jax.random.split(key, 26)
    f32 = jnp.float32
    def nrm(k, shape, s):
        return jax.random.normal(k, shape, f32) * s
    n_pages = PAST_LEN // PAGE_SIZE
    n_phys = (DEC_BATCH * n_pages * 5) // 4
    wb = min(WINDOW, PAST_LEN)
    page_table = jax.random.permutation(ks[5], n_phys)[:DEC_BATCH * n_pages].reshape(DEC_BATCH, n_pages).astype(jnp.int32)
    return {
        'x_prompt': nrm(ks[0], (BATCH, SEQ, D_MODEL), 1.0),
        'x_sample': nrm(ks[1], (DEC_BATCH, DEC_SEQ, D_MODEL), 1.0),
        'cache_nsa': nrm(ks[2], (DEPTH, n_phys, PAGE_SIZE, N_KV_SEL, G_A, HD_A), 1.0),
        'cache_mla': nrm(ks[3], (DEPTH, n_phys, PAGE_SIZE, KV_LORA + ROPE_DIM), 1.0),
        'state_win': nrm(ks[4], (DEPTH, DEC_BATCH, wb, 2, G_A, HD_A), 1.0),
        'page_table': page_table,
        'c_prompt': nrm(ks[6], (BATCH, D_MODEL), 1.0),
        'c_sample': nrm(ks[7], (DEC_BATCH, D_MODEL), 1.0),
        'w_ada': nrm(ks[8], (DEPTH, D_MODEL, 3 * D_MODEL), 0.5 * D_MODEL ** -0.5),
        'b_ada': nrm(ks[9], (DEPTH, 3 * D_MODEL), 0.02),
        'g_norm': 1.0 + nrm(ks[10], (DEPTH, D_MODEL), 0.01),
        'w_in': nrm(ks[11], (DEPTH, D_MODEL, N_IN), D_MODEL ** -0.5),
        'w_cmp_k': nrm(ks[12], (DEPTH, CMP_BLOCK, HD_A, HD_A), (CMP_BLOCK * HD_A) ** -0.5),
        'w_cmp_v': nrm(ks[13], (DEPTH, CMP_BLOCK, HD_A, HD_A), (CMP_BLOCK * HD_A) ** -0.5),
        'pe_cmp_k': nrm(ks[14], (DEPTH, CMP_BLOCK, HD_A), 0.1),
        'pe_cmp_v': nrm(ks[15], (DEPTH, CMP_BLOCK, HD_A), 0.1),
        'rel_bias': nrm(ks[16], (N_BUCKETS, H_A), 0.1),
        'g_q_lat': 1.0 + nrm(ks[17], (DEPTH, Q_LORA), 0.01),
        'w_uq': nrm(ks[18], (DEPTH, Q_LORA, H_B, NOPE + ROPE_DIM), Q_LORA ** -0.5),
        'g_kv_lat': 1.0 + nrm(ks[19], (DEPTH, KV_LORA), 0.01),
        'w_uk': nrm(ks[20], (DEPTH, KV_LORA, H_B, NOPE), KV_LORA ** -0.5),
        'w_uv': nrm(ks[21], (DEPTH, KV_LORA, H_B, V_HEAD), KV_LORA ** -0.5),
        'w_out': nrm(ks[22], (DEPTH, W_A + W_B, D_MODEL), (W_A + W_B) ** -0.5),
        'g_final': 1.0 + nrm(ks[23], (D_MODEL,), 0.01),
    }

def reference(x_prompt, x_sample, cache_nsa, cache_mla, state_win, page_table, c_prompt, c_sample,
              w_ada, b_ada, g_norm, w_in, w_cmp_k, w_cmp_v, pe_cmp_k, pe_cmp_v, rel_bias,
              g_q_lat, w_uq, g_kv_lat, w_uk, w_uv, w_out, g_final):
    xp, xs = x_prompt, x_sample
    nsa_p, nsa_s, mla_p, mla_s, win_p, win_s = [], [], [], [], [], []
    for l in range(DEPTH):
        lw = (w_ada[l], b_ada[l], g_norm[l], w_in[l], g_q_lat[l], w_uq[l], g_kv_lat[l], w_uk[l])
        cw = (w_cmp_k[l], w_cmp_v[l], pe_cmp_k[l], pe_cmp_v[l])
        xp, rows_n, rows_m, rows_w = prompt_layer(xp, c_prompt, lw, cw, rel_bias, w_uv[l], w_out[l])
        nsa_p.append(rows_n)
        mla_p.append(rows_m)
        win_p.append(rows_w)
        xs, rows_n, rows_m, rows_w = sample_layer(xs, c_sample, cache_nsa[l], cache_mla[l], state_win[l],
                                                  page_table, lw, cw, rel_bias, w_uv[l], w_out[l])
        nsa_s.append(rows_n)
        mla_s.append(rows_m)
        win_s.append(rows_w)
    y_prompt = rmsnorm(xp, g_final)
    y_sample = rmsnorm(xs, g_final)
    return (y_prompt, y_sample, jnp.stack(nsa_p), jnp.stack(nsa_s), jnp.stack(mla_p), jnp.stack(mla_s),
            jnp.stack(win_p), jnp.stack(win_s))


_drawn_inputs = setup_inputs


def setup_inputs(seed=0):
    import zlib

    import numpy as np

    out = dict(_drawn_inputs(seed))
    spreads = {}
    factors = {'cache_mla': 5.843,
     'g_norm': 6.338,
     'pe_cmp_k': 8.0,
     'pe_cmp_v': 3.358,
     'rel_bias': 8.0,
     'g_q_lat': 8.0,
     'g_kv_lat': 7.823,
     'g_final': 5.803}
    for name, (base, spread) in spreads.items():
        noise = np.random.default_rng([zlib.crc32(name.encode()), seed]).standard_normal(out[name].shape)
        drawn = base * np.exp(spread * noise) if base else spread * noise
        out[name] = __import__('jax').numpy.asarray(drawn.astype(out[name].dtype))
    for name, factor in factors.items():
        out[name] = (out[name] * factor).astype(out[name].dtype)
    return out
```

```python
from contextlib import ExitStack

import numpy as np
import concourse.bass as bass
from concourse import mybir

F32 = mybir.dt.float32
I32 = mybir.dt.int32
ACT = mybir.ActivationFunctionType
ALU = mybir.AluOpType
AX = mybir.AxisListType.X

P = 128
DM = 1024
KT = DM // P
SEQ = 1024
NT = SEQ // P
NB = 8
TS = 4
RS = NB * TS
PAST = 2048
NPG = PAST // P
NPHYS = 160
G, R, HD = 2, 4, 64
H = G * R
ROPE = 64
LAT = 128
HB = 4
W1N = 1304
W2N = 1472
NCH_P, NCH_S = 64, 128
NCMP_P, NCMP_S = NCH_P - 1, NCH_S - 1
NSB = 33
NFREE = 30
KEEP = 13
BIG = -1e30
MSC = float(192) ** -0.5
EPS = 1e-6


def _bucket(n):
    n = max(int(n), 0)
    if n < 16:
        return n
    return min(31, 16 + int(np.log(n / 16.0) / np.log(8.0) * 16))


def constants():
    a = np.arange(P)
    ident = np.eye(P, dtype=np.float32)
    flip = ident[::-1].copy()
    wmask = np.where(a[None, :] > a[:, None], 0.0, BIG).astype(np.float32)
    cmask = np.where(a[None, :] <= a[:, None], 0.0, BIG).astype(np.float32)
    inv = (10000.0 ** (-np.arange(32) / 32.0)).astype(np.float32)

    def rope(pos):
        ang = (pos.astype(np.float32)[:, None] * inv[None, :]).astype(np.float32).astype(np.float64)
        c, s = np.cos(ang), np.sin(ang)
        return (np.concatenate([c, c], 1).astype(np.float32), np.concatenate([-s, s], 1).astype(np.float32))

    c, s = rope(np.arange(SEQ))
    cosp = c.reshape(NT, P, 64).transpose(1, 0, 2).reshape(P, -1)
    sinp = s.reshape(NT, P, 64).transpose(1, 0, 2).reshape(P, -1)
    half = np.full((P, 1), -0.5, np.float32)
    cA = np.concatenate([ident, flip, wmask, cmask, half], 1)
    cF = np.concatenate([cosp, sinp], 1)

    def onehot(dists):
        m = np.zeros((33, len(dists)), np.float32)
        for y, d in enumerate(dists):
            if d < 0:
                m[32, y] = BIG
            else:
                m[_bucket(d), y] += 1.0
                m[31, y] -= 1.0
        return m

    cB = np.concatenate([onehot([255 - y for y in range(383)]), onehot([x - 127 for x in range(383)])], 1)
    cs = np.arange(NCMP_S)[:, None] * 16
    ss = np.arange(NSB)[None, :] * 64
    ov = np.maximum(np.minimum(cs + 32, ss + 64) - np.maximum(cs, ss), 0).astype(np.float32) / 32
    rows = np.arange(RS)
    cr, sr = rope(PAST + rows % TS)
    bd = ((rows[:, None] // 16) == (np.arange(P)[None, :] // 64)).astype(np.float32)
    fold = ((rows[:, None] % 16) == np.arange(16)[None, :]).astype(np.float32)
    t = rows[:, None] % TS
    c4 = np.arange(TS)[None, :]
    wm = np.where(c4 <= t, BIG, 0.0).astype(np.float32)
    cm = np.where(c4 <= t, 0.0, BIG).astype(np.float32)
    j = np.arange(NFREE)
    low = np.broadcast_to((j[None, :] < j[:, None]).astype(np.float32).reshape(1, -1), (RS, NFREE * NFREE))
    cD = np.concatenate([cr, sr, bd, fold, wm, cm, low], 1)
    return {k: np.ascontiguousarray(v, np.float32) for k, v in
            {"cA": cA, "cB": cB, "cC": ov, "cD": cD, "cF": cF}.items()}


def build(nc, x_prompt, x_sample, cache_nsa, cache_mla, state_win, page_table, c_prompt, c_sample,
          w_ada, b_ada, g_norm, w_in, w_cmp_k, w_cmp_v, pe_cmp_k, pe_cmp_v, rel_bias,
          g_q_lat, w_uq, g_kv_lat, w_uk, w_uv, w_out, g_final, cA, cB, cC, cD, cF,
          y_prompt, y_sample, nsa_p, nsa_s, mla_p, mla_s, win_p, win_s):
    with ExitStack() as ctx:
        def sb(name, shape, dt=F32):
            return ctx.enter_context(nc.sbuf_tensor(name, shape, dt))

        def sem(name):
            return ctx.enter_context(nc.semaphore(name))

        def sems(name, n):
            return [sem(f"{name}{i}") for i in range(n)]

        U_dram = nc.dram_tensor("rel_by_distance", (H, 383), F32, kind="Internal").ap()
        gate_dram = nc.dram_tensor("gate_rows", (9, DM), F32, kind="Internal").ap()
        gs_dram = nc.dram_tensor("branch_gates", (RS, 24), F32, kind="Internal").ap()

        PS = ctx.enter_context(nc.psum_tensor("PS", [P, 8, 512], F32))

        CA = sb("CA", [P, 4 * P + 1])
        CC = sb("CC", [NCMP_S, NSB])
        CD = sb("CD", [RS, 64 + 64 + 128 + 16 + 4 + 4 + 900])
        PT_SB = sb("PT_SB", [1, NB * NPG], I32)
        ident, flip = CA[:, 0:128], CA[:, 128:256]
        wmask, cmask, mhalf = CA[:, 256:384], CA[:, 384:512], CA[:, 512:513]
        cosS, sinS, bdm, foldm = CD[:, 0:64], CD[:, 64:128], CD[:, 128:256], CD[:, 256:272]
        wmS, cmS, lowS = CD[:, 272:276], CD[:, 276:280], CD[:, 280:1180]

        AR = sb("AR", [P, 49440])

        def view(off, n):
            return AR[:, off:off + n]

        Z = view(0, 8192).rearrange("p (i c) -> p i c", i=NT)
        CQT = view(8192, 2048).rearrange("p (k t) -> p k t", k=2)
        QT = view(10432, 4096).rearrange("p (r t) -> p r t", r=R)
        KSELT, KWINT, CKVT, KRT = (view(14528 + 1024 * n, 1024) for n in range(4))
        VSEL = view(18624, 1024).rearrange("p (i c) -> p i c", i=NT)
        CKV = view(19648, 1024).rearrange("p (i c) -> p i c", i=NT)
        KVWIN = view(20672, 2048).rearrange("p (i c) -> p i c", i=NT)
        GAT = view(22720, 192).rearrange("p (i c) -> p i c", i=NT)
        W1 = view(0, KT * W1N).rearrange("p (k n) -> p k n", k=KT)
        HT = view(22912, 8192).rearrange("p (i k t) -> p i k t", i=NT, k=KT)
        HTS = view(31104, 256).rearrange("p (k t) -> p k t", k=KT)
        W2 = view(31360, KT * W2N).rearrange("p (k n) -> p k n", k=KT)
        ADA = [view(31360 + 3072 * n, 3072) for n in range(3)]
        XS = [view(43136 + 1024 * n, 1024) for n in range(2)]
        SLA = [view(45184 + 512 * n, 512) for n in range(2)]
        SLD = [view(46208 + 448 * n, 448) for n in range(2)]
        WNS = view(46208, 256)
        ZNS = view(45184, 1024)
        RT = [view(43136 + 128 * n, 128) for n in range(2)]
        COSSIN = view(43648, 1024).rearrange("p (a i c) -> p a i c", a=2, i=NT)
        MODR = view(14528, 3072)
        CT = view(17600, 72).rearrange("p (k c) -> p k c", k=KT)
        CB = view(17700, 766)
        US = view(18470, 383)
        CROW = view(45184, 1024)
        GST = view(46208, 128)
        BADA = view(22912, 3072)
        KCVP = view(22912, 4096).rearrange("p (l c) -> p l c", l=16)
        KCPP = view(27008, 4096).rearrange("p (c l d) -> p c l d", c=4, l=16)
        XTP = view(31104, 2048).rearrange("p (c l n) -> p c l n", c=2, l=8)
        RBP = view(40448, 256).rearrange("p (c n) -> p c n", c=2)
        QLATT = view(22912, 4096).rearrange("p (h t) -> p h t", h=HB)
        QRT = view(27008, 4096).rearrange("p (h t) -> p h t", h=HB)
        BT = view(31104, 2048).rearrange("p (h c) -> p h c", h=H)
        PB = [view(33280 + 1024 * n, 1024) for n in range(2)]
        TT = view(33280, 2048).rearrange("p (h c) -> p h c", h=H)
        PTB = [view(35328 + 1024 * n, 1024).rearrange("p (k q) -> p k q", k=8) for n in range(2)]
        QSH = [view(37376, 1024), view(42112, 1024)]
        QLH, QRH = view(38400, 1024), view(39424, 1024)
        YACC = view(40448, 1024).rearrange("p (i g d) -> p i g d", i=NT, g=G)
        WUV = view(41472, 512).rearrange("p (h v) -> p h v", h=HB)
        OTB = [view(43136 + 128 * n, 128) for n in range(2)]
        WUQ = view(42112, 1536).rearrange("p (k h e) -> p k h e", k=2, h=HB)
        WLAT = view(45184, 1024).rearrange("p (k h r) -> p k h r", k=2, h=HB)
        WUK = view(35328, 512).rearrange("p (h n) -> p h n", h=HB)
        WT = view(35840, 1536).rearrange("p (h m) -> p h m", h=HB)
        QRN = [view(37376 + 512 * n, 256) for n in range(2)]
        QRM = [view(38400 + 512 * n, 256) for n in range(2)]
        WC = view(47104, 2048).rearrange("p (c l m) -> p c l m", c=2, l=8)
        tail = [49152]

        def kept(n):
            tail[0] += n
            assert tail[0] <= 49440
            return view(tail[0] - n, n)

        QTS = kept(128).rearrange("p (r t) -> p r t", r=R)
        KSELTS, KWINTS, CKVTS, KRTS = kept(32), kept(32), kept(32), kept(32)
        SM_ = sb("SM_", [P, 1648])
        cur = [0]

        def small(n):
            cur[0] += n
            assert cur[0] <= 1648
            return SM_[:, cur[0] - n:cur[0]]

        ZTS = small(256).rearrange("p (f t) -> p f t", f=8)
        QLTS = small(128).rearrange("p (h t) -> p h t", h=HB)
        QRTS = small(128).rearrange("p (h t) -> p h t", h=HB)
        CQTS = small(64).rearrange("p (k t) -> p k t", k=2)
        MODT = small(144).rearrange("p (k c) -> p k c", k=16)
        GNT, GQT, GKV = small(8), small(2), small(128)
        BC = small(120).rearrange("p (n h) -> p n h", n=15)
        RBA = small(8)
        ONE9 = small(9)
        SSQ, RSTD = small(9), small(9)
        SSQ2 = small(18).rearrange("p (j c) -> p j c", c=2)
        RSTD2 = small(18).rearrange("p (j c) -> p j c", c=2)
        GATS = small(24)
        GBS = small(24).rearrange("p (b c) -> p b c", b=NB)
        CCON = small(2)
        PET = small(32).rearrange("p (c l s) -> p c l s", c=2, l=8)
        NM = small(4).rearrange("p (s g) -> p s g", s=2)
        SU = small(16).rearrange("p (s g) -> p s g", s=8)
        RC = small(2)
        CF = small(2)
        KCTP = small(63)
        VCP = small(128)

        s_cst, s_cnd, s_gv, s_ones = sem("s_cst"), sem("s_cnd"), sem("s_gv"), sem("s_ones")
        s_ada, s_adak = sems("s_ada", 3), sem("s_adak")
        s_w1, s_w2 = sem("s_w1"), sem("s_w2")
        s_ct, s_ctv = sem("s_ct"), sem("s_ctv")
        s_mod, s_modA, s_modD = sem("s_mod"), sem("s_modA"), sem("s_modD")
        s_u, s_us, s_bc, s_udma, s_gdma = sem("s_u"), sem("s_us"), sem("s_bc"), sem("s_udma"), sem("s_gdma")
        s_mt, s_modt = sem("s_mt"), sem("s_modt")
        s_x = sems("s_x", 2)
        s_ssq, s_ms, s_rstd, s_xn, s_xt = sem("s_ssq"), sem("s_ms"), sem("s_rstd"), sem("s_xn"), sem("s_xt")
        s_hA, s_hD, s_hm = sem("s_hA"), sem("s_hD"), sem("s_hm")
        s_q, s_A, s_B = sem("s_q"), sem("s_A"), sem("s_B")
        s_qe, s_Ae, s_Be, s_tg, s_gate = sem("s_qe"), sem("s_Ae"), sem("s_Be"), sem("s_tg"), sem("s_gate")
        s_vs, s_oA, s_kT, s_kTe = sem("s_vs"), sems("s_oA", 2), sem("s_kT"), sem("s_kTe")
        s_oW, s_gs, s_gsb = sem("s_oW"), sem("s_gs"), sem("s_gsb")
        s_cos = sem("s_cos")
        s_C, s_D, s_E = sem("s_C"), sem("s_D"), sem("s_E")
        s_tC, s_tE, s_zC, s_zE = sem("s_tC"), sem("s_tE"), sem("s_zC"), sem("s_zE")
        s_sq2, s_ms2, s_rs2 = sem("s_sq2"), sem("s_ms2"), sem("s_rs2")
        s_cqn, s_ckv, s_r1, s_r2, s_kr = sem("s_cqn"), sem("s_ckv"), sem("s_r1"), sem("s_r2"), sem("s_kr")
        s_cc, s_oD, s_dT, s_dTe = sem("s_cc"), sems("s_oD", 2), sem("s_dT"), sem("s_dTe")
        s_zT, s_zTe = sem("s_zT"), sem("s_zTe")
        s_p2 = sem("s_p2")

        IDX = list(range(9))

        def rows(j):
            return RS if j == 0 else P

        def ht(j, k):
            return HTS[:, k, :] if j == 0 else HT[:, j - 1, k, :]

        def tok(j):
            return slice(P * (j - 1), P * j)

        w_in2 = w_in[0].rearrange("(k p) n -> p k n", p=P)
        x_t = [x_sample.rearrange("b t d -> (b t) d")] + [x_prompt[0, P * i:P * i + P, :] for i in range(NT)]
        nsa_t = [nsa_s.rearrange("l b t c g d -> (l b t) (c g d)")] + \
                [nsa_p[0, 0, P * i:P * i + P].rearrange("t c g d -> t (c g d)") for i in range(NT)]
        mla_t = [mla_s.rearrange("l b t c -> (l b t) c")] + [mla_p[0, 0, P * i:P * i + P, :] for i in range(NT)]

        def w1q(k, r):
            return W1[:, k, P * r:P * r + P]

        def w2cols(k, lo, hi):
            if lo == 0:
                return W2[:, k, 0:512].rearrange("p (g r d) -> p r g d", g=G, r=R)
            return W2[:, k, lo:hi]

        def sp_projection(sp):
            sp.dma_start(CROW[0:8, :], c_sample).then_inc(s_cnd, 16)
            sp.dma_start(CROW[8:9, :], c_prompt).then_inc(s_cnd, 16)
            sp.dma_start(CA[:], cA).then_inc(s_cst, 16)
            sp.dma_start(GST[0:8, :], g_norm[0].rearrange("(k p) -> k p", p=P)).then_inc(s_gv, 16)
            sp.dma_start(GST[8:10, :], g_q_lat[0].rearrange("(k p) -> k p", p=P)).then_inc(s_gv, 16)
            sp.dma_start(BADA[0:1, :], b_ada).then_inc(s_gv, 16)
            ada_v = w_ada[0].rearrange("(k p) n -> k p n", p=P)
            for k in range(3):
                sp.dma_start(ADA[k], ada_v[k]).then_inc(s_ada[k], 16)
            sp.dma_start(RBA[0:32, :], rel_bias).then_inc(s_cst, 16)
            sp.dma_start(CB[0:33, :], cB).then_inc(s_cst, 16)
            sp.dma_start(CC[:], cC).then_inc(s_cst, 16)
            sp.dma_start(CD[:], cD).then_inc(s_cst, 16)
            sp.dma_start(GKV, g_kv_lat.to_broadcast([P, P])).then_inc(s_cst, 16)
            sp.dma_start(PT_SB[:], page_table.rearrange("b n -> (b n)").rearrange("(a m) -> a m", a=1))\
                .then_inc(s_cst, 16)
            for k in range(3, KT):
                sp.wait_ge(s_adak, k - 2)
                sp.dma_start(ADA[k % 3], ada_v[k]).then_inc(s_ada[k % 3], 16)
            for j in range(2):
                sp.dma_start(XS[j][0:rows(j), :], x_t[j]).then_inc(s_x[j], 16)
            sp.dma_start(W1[:, :, 512:W1N], w_in2[:, :, 512:W1N]).then_inc(s_w1, 16)
            for k in range(KT):
                for g in range(G):
                    sp.dma_start(W1[:, k, 0:512].rearrange("p (r g d) -> p r g d", r=R, g=G)[:, :, g, :],
                                 w_in2[:, k, 256 * g:256 * g + 256].rearrange("p (r d) -> p r d", r=R))\
                        .then_inc(s_w1, 16)
            sp.wait_ge(s_us, 1)
            sp.dma_start(U_dram, US[0:8, :]).then_inc(s_udma, 16)
            sp.wait_ge(s_modA, 3)
            sp.wait_ge(s_modD, 3)
            sp.dma_start(gate_dram, MODR[0:9, 2048:3072]).then_inc(s_gdma, 16)
            sp.wait_ge(s_adak, KT)
            sp.dma_start(W2[:, :, :], w_in2[:, :, W1N:W1N + W2N]).then_inc(s_w2, 16)
            for c, (w, pe_) in enumerate(((w_cmp_k, pe_cmp_k), (w_cmp_v, pe_cmp_v))):
                wv = w[0].rearrange("(s l q) d e -> s (q d) l e", s=2, q=2)
                pv = pe_[0].rearrange("(s l q) d -> s (q d) l", s=2, q=2)
                for s in range(2):
                    sp.dma_start(WC[:, c, :, 64 * s:64 * s + 64], wv[s]).then_inc(s_cc, 16)
                    sp.dma_start(PET[:, c, :, s], pv[s], allow_slow_non_contiguous=True).then_inc(s_cc, 16)
            for j in IDX:
                if j + 2 <= 8:
                    sp.wait_ge(s_xt, j + 1)
                    sp.dma_start(XS[j % 2], x_t[j + 2]).then_inc(s_x[j % 2], 16)
                sp.wait_ge(s_Ae, j + 1)
                sp.dma_start(nsa_t[j], SLA[j % 2][0:rows(j), :]).then_inc(s_oA[j % 2], 16)
                if j == 0:
                    sp.wait_ge(s_Be, 1)
                    for b in range(NB):
                        sp.dma_start(win_s[0, b, 508:512].rearrange("t c g d -> t (c g d)"),
                                     WNS[4 * b:4 * b + 4, :]).then_inc(s_oW, 16)
                    sp.wait_ge(s_gate, 1)
                    sp.dma_start(gs_dram, GATS[0:RS, :]).then_inc(s_gs, 16)
            sp.wait_ge(s_Be, 9)
            sp.dma_start(win_p[0, 0].rearrange("(i p) c g d -> p i (c g d)", p=P), KVWIN[:, 4:8, :])\
                .then_inc(s_oW, 16)
            sp.wait_ge(s_xt, 9)
            sp.dma_start(COSSIN, cF.rearrange("p (a i c) -> p a i c", a=2, i=NT)).then_inc(s_cos, 16)
            sp.wait_ge(s_gs, 16)
            for h in range(H):
                sp.dma_start(GBS[4 * h:4 * h + 4, :, :],
                             gs_dram.rearrange("(b t) c -> t b c", b=NB)[:, :, 3 * h:3 * h + 3]).then_inc(s_gsb, 16)
            for j in IDX:
                sp.wait_ge(s_kr, j + 1)
                sp.dma_start(mla_t[j], SLD[j % 2][0:rows(j), 256:448]).then_inc(s_oD[j % 2], 16)

        def pe_projection(pe):
            pe.wait_ge(s_cst, 16 * 7)
            pe.wait_ge(s_cnd, 32)
            pe.wait_ge(s_gv, 48)
            for k in range(KT):
                pe.transpose(PS[:, 0, 9 * k:9 * k + 9], CROW[0:9, P * k:P * k + P], ident[0:9, 0:9])
            pe.transpose(PS[:, 0, 80:90], GST[0:10, :], ident[0:10, 0:10]).then_inc(s_ct, 1)
            pe.wait_ge(s_ctv, 3)
            for k in range(KT):
                pe.wait_ge(s_ada[k % 3], 16 * (k // 3 + 1))
                for n in range(6):
                    mm = pe.matmul(PS[0:9, 1 + n, :], CT[:, k, :], ADA[k % 3][:, 512 * n:512 * n + 512],
                                   start=(k == 0), stop=False)
                mm.then_inc(s_adak, 1)
            pe.wait_ge(s_ones, 2)
            for n in range(6):
                pe.matmul(PS[0:9, 1 + n, :], ONE9[0:1, :], BADA[0:1, 512 * n:512 * n + 512],
                          start=False, stop=True).then_inc(s_mod, 1)
            pe.matmul(PS[0:8, 7, 0:383], RBA[0:33, :], CB[0:33, 0:383], start=True, stop=True).then_inc(s_u, 1)
            for n in range(15):
                mm = pe.matmul(PS[:, 0, 8 * n:8 * n + 8], CB[0:33, 383 + 16 * (14 - n):383 + 16 * (14 - n) + P],
                               RBA[0:33, :], start=True, stop=True)
            mm.then_inc(s_u, 1)
            pe.wait_ge(s_modA, 3)
            pe.wait_ge(s_modD, 3)
            for n in range(16):
                mm = pe.transpose(PS[:, 1, 9 * n:9 * n + 9], MODR[0:9, P * n:P * n + P], ident[0:9, 0:9])
            mm.then_inc(s_mt, 1)
            pe.wait_ge(s_bc, 1)
            pe.wait_ge(s_modt, 2)
            for j in IDX:
                n = rows(j)
                pe.wait_ge(s_xn, j + 1)
                if j >= 1:
                    pe.wait_ge(s_hA, j)
                    pe.wait_ge(s_hD, j)
                for k in range(KT):
                    mm = pe.transpose(PS[:, k // 4, P * (k % 4):P * (k % 4) + n],
                                      XS[j % 2][0:n, P * k:P * k + P], ident[0:n, 0:n])
                mm.then_inc(s_xt, 1)
                if j >= 1:
                    pe_keys(pe, j - 1)
                if j == 0:
                    pe.wait_ge(s_w1, 16 * (1 + 2 * KT))
                pe.wait_ge(s_hA, j + 1)
                pe.wait_ge(s_hD, j + 1)
                if j >= 1:
                    pe.wait_ge(s_qe, j)
                for r in range(R):
                    for k in range(KT):
                        mm = pe.matmul(PS[:, 2, P * r:P * r + n], w1q(k, r), ht(j, k)[:, 0:n],
                                       start=(k == 0), stop=(k == KT - 1))
                mm.then_inc(s_q, 1)
                if j >= 1:
                    pe.wait_ge(s_Ae, j)
                for k in range(KT):
                    mm = pe.matmul(PS[0:n, 3, :], ht(j, k)[:, 0:n], W1[:, k, 512:1024],
                                   start=(k == 0), stop=(k == KT - 1))
                mm.then_inc(s_A, 1)
                if j >= 1:
                    pe.wait_ge(s_Be, j)
                    pe.wait_ge(s_tg, j)
                for k in range(KT):
                    mm = pe.matmul(PS[0:n, 4, 0:280], ht(j, k)[:, 0:n], W1[:, k, 1024:1304],
                                   start=(k == 0), stop=(k == KT - 1))
                mm.then_inc(s_B, 1)
            pe_keys(pe, 8)
            pe.wait_ge(s_w2, 16)
            for j in IDX:
                n = rows(j)
                if j == 0:
                    pe.wait_ge(s_qe, 9)
                    pe.wait_ge(s_Ae, 9)
                    pe.wait_ge(s_Be, 9)
                    pe.wait_ge(s_tg, 9)
                for bank, lo, hi, done, free in ((3, 512, 960, s_D, s_kr), (2, 0, 512, s_C, s_zC),
                                                 (4, 960, 1472, s_E, s_zE)):
                    if j >= 1:
                        pe.wait_ge(free, j)
                    for k in range(KT):
                        mm = pe.matmul(PS[0:n, bank, 0:hi - lo], ht(j, k)[:, 0:n], w2cols(k, lo, hi),
                                       start=(k == 0), stop=(k == KT - 1))
                    mm.then_inc(done, 1)
                if j >= 1:
                    pe_latents(pe, j - 1)
            pe_latents(pe, 8)
            pe.wait_ge(s_zC, 1)
            pe.wait_ge(s_zE, 1)
            pe.wait_ge(s_hA, 9)
            for f in range(8):
                mm = pe.transpose(PS[:, 0, RS * f:RS * f + RS], ZNS[0:RS, P * f:P * f + P], ident[0:RS, 0:RS])
            mm.then_inc(s_zT, 1)

        def pe_keys(pe, j):
            n = rows(j)
            pe.wait_ge(s_Ae, j + 1)
            pe.wait_ge(s_Be, j + 1)
            if j >= 1:
                pe.wait_ge(s_kTe, 2 * j)
            pe.transpose(PS[:, 5, 0:n], SLA[j % 2][0:n, 256:384], ident[0:n, 0:n])
            win = WNS[0:n, 0:128] if j == 0 else KVWIN[:, j - 1, 0:128]
            pe.transpose(PS[:, 5, 128:128 + n], win, ident[0:n, 0:n]).then_inc(s_kT, 1)

        def pe_latents(pe, j):
            n = rows(j)
            pe.wait_ge(s_kr, j + 1)
            if j >= 1:
                pe.wait_ge(s_dTe, 3 * j)
            else:
                pe.wait_ge(s_kTe, 18)
            for k in range(2):
                pe.transpose(PS[:, 5, P * k:P * k + n], SLD[j % 2][0:n, P * k:P * k + P], ident[0:n, 0:n])
            pe.transpose(PS[:, 5, 256:256 + n], SLD[j % 2][0:n, 256:384], ident[0:n, 0:n])
            pe.transpose(PS[0:64, 6, 0:n], SLD[j % 2][0:n, 384:448], ident[0:n, 0:n]).then_inc(s_dT, 1)

        def act_projection(act):
            for n in (0, 2, 4):
                act.wait_ge(s_mod, n + 1)
                act.activation(MODR[0:9, 512 * n:512 * n + 512], PS[0:9, 1 + n, :], ACT.Copy).then_inc(s_modA, 1)
            act.wait_ge(s_u, 1)
            act.activation(US[0:8, :], PS[0:8, 7, 0:383], ACT.Copy).then_inc(s_us, 1)
            act.wait_ge(s_ms, 1)
            for j in IDX:
                n = rows(j)
                act.wait_ge(s_x[j % 2], 16 * (j // 2 + 1))
                junk = HT[0:n, 7 if j == 0 else j - 1, :, :].rearrange("p k t -> p (k t)")
                if j == 0:
                    act.wait_ge(s_mod, 6)
                act.activation(junk, XS[j % 2][0:n, :], ACT.Square, accum_out=SSQ[0:n, j:j + 1]).then_inc(s_ssq, 1)
                act.wait_ge(s_ssq, j + 1)
                act.wait_ge(s_xt, j + 1)
                act.wait_ge(s_modt, 2)
                if j == 0:
                    act.activation(CCON[0:1, 0:1], ONE9[0:1, 0:1], ACT.Copy).then_inc(s_hA, 1)
                else:
                    for k in range(4):
                        ins = act.activation(HT[:, j - 1, k, :], PS[:, k // 4, P * (k % 4):P * (k % 4) + P],
                                             ACT.Identity, bias=MODT[:, k, 8:9], scale=MODT[:, 8 + k, 8:9])
                    ins.then_inc(s_hA, 1)
                act.wait_ge(s_q, j + 1)
                dst = QTS[:, :, :] if j == 0 else QT[:, :, tok(j)]
                act.activation(dst, PS[:, 2, :].rearrange("p (r t) -> p r t", r=R)[:, :, 0:n],
                               ACT.Copy, scale=0.125).then_inc(s_qe, 1)
                act.wait_ge(s_A, j + 1)
                if j >= 2:
                    act.wait_ge(s_oA[j % 2], 16 * (j // 2))
                    act.wait_ge(s_vs, j - 1)
                    act.wait_ge(s_kT, j - 1)
                act.activation(SLA[j % 2][0:n, :], PS[0:n, 3, :], ACT.Copy).then_inc(s_Ae, 1)
                act.wait_ge(s_Be, j + 1)
                gat = GATS[0:n, :] if j == 0 else GAT[:, j - 1, :]
                act.activation(gat, PS[0:n, 4, 256:280], ACT.Tanh, scale=0.5).then_inc(s_tg, 1)
            for j in IDX:
                n = rows(j)
                act.wait_ge(s_D, j + 1)
                junk = RT[0]
                zb = ZNS[0:n, :] if j == 0 else Z[:, j - 1, :]
                if j == 0:
                    act.wait_ge(s_oA[0], 16 * 5)
                    act.wait_ge(s_oA[1], 16 * 4)
                    act.wait_ge(s_vs, 9)
                    act.wait_ge(s_kT, 9)
                    act.wait_ge(s_B, 9)
                act.activation(zb[:, 0:256], PS[0:n, 3, 0:256], ACT.Square,
                               accum_out=SSQ2[0:n, j, 0:1])
                act.activation(zb[:, 256:384], PS[0:n, 3, 256:384], ACT.Square,
                               accum_out=SSQ2[0:n, j, 1:2]).then_inc(s_sq2, 1)
                act.wait_ge(s_sq2, j + 1)
                act.wait_ge(s_C, j + 1)
                act.activation(zb[:, 0:512], PS[0:n, 2, :], ACT.Tanh, scale=0.5).then_inc(s_tC, 1)
                act.wait_ge(s_E, j + 1)
                act.activation(zb[:, 512:1024], PS[0:n, 4, :], ACT.Tanh, scale=0.5).then_inc(s_tE, 1)
            act.wait_ge(s_zT, 1)
            act.activation(ZTS, PS[:, 0, 0:256].rearrange("p (f t) -> p f t", f=8), ACT.Copy).then_inc(s_zTe, 1)

        def dve_projection(dve):
            dve.wait_ge(s_ct, 1)
            dve.tensor_copy(CT, PS[:, 0, 0:72].rearrange("p (k c) -> p k c", k=KT)).then_inc(s_ctv, 1)
            dve.tensor_copy(GNT, PS[:, 0, 80:88]).then_inc(s_ctv, 1)
            dve.tensor_copy(GQT, PS[:, 0, 88:90]).then_inc(s_ctv, 1)
            for n in (1, 3, 5):
                dve.wait_ge(s_mod, n + 1)
                dve.tensor_copy(MODR[0:9, 512 * n:512 * n + 512], PS[0:9, 1 + n, :]).then_inc(s_modD, 1)
            dve.wait_ge(s_u, 2)
            dve.tensor_copy(BC, PS[:, 0, 0:120].rearrange("p (n h) -> p n h", n=15)).then_inc(s_bc, 1)
            dve.wait_ge(s_mt, 1)
            dve.wait_ge(s_ctv, 3)
            mt = PS[:, 1, 0:144].rearrange("p (k c) -> p k c", k=16)
            dve.tensor_copy(MODT[:, 0:8, :], mt[:, 0:8, :]).then_inc(s_modt, 1)
            dve.scalar_tensor_tensor(MODT[:, 8:16, :], mt[:, 8:16, :], 1.0,
                                     GNT.rearrange("p (k c) -> p k c", c=1).to_broadcast([P, 8, 9]),
                                     ALU.add, ALU.mult).then_inc(s_modt, 1)
            for j in IDX:
                n = rows(j)
                dve.wait_ge(s_rstd, j + 1)
                dve.tensor_scalar(XS[j % 2][0:n, :], XS[j % 2][0:n, :], RSTD[0:n, j:j + 1], None, ALU.mult)\
                    .then_inc(s_xn, 1)
                dve.wait_ge(s_xt, j + 1)
                if j == 0:
                    dve.wait_ge(s_modt, 2)
                    for f in range(2):
                        src = PS[:, f, :].rearrange("p (k t) -> p k t", k=4)[:, :, 0:RS]\
                            .rearrange("p k (b t) -> p k b t", b=NB)
                        dst = HTS[:, 4 * f:4 * f + 4, :].rearrange("p k (b t) -> p k b t", b=NB)
                        for half, op in ((8, ALU.mult), (0, ALU.add)):
                            m = MODT[:, half + 4 * f:half + 4 * f + 4, 0:8]\
                                .rearrange("p k (b t) -> p k b t", t=1).to_broadcast([P, 4, NB, TS])
                            ins = dve.tensor_tensor(dst, src, m, op)
                            src = dst
                            if half:
                                ins.then_inc(s_hm, 1)
                                dve.wait_ge(s_hm, f + 1)
                    ins.then_inc(s_hD, 1)
                else:
                    for k in range(4, KT):
                        ins = dve.tensor_scalar(HT[:, j - 1, k, :], PS[:, k // 4, P * (k % 4):P * (k % 4) + P],
                                                MODT[:, 8 + k, 8:9], MODT[:, k, 8:9], ALU.mult, ALU.add)
                    ins.then_inc(s_hD, 1)
                if j >= 1:
                    dve_keys(dve, j - 1)
                dve.wait_ge(s_B, j + 1)
                if j == 0:
                    dve.tensor_copy(WNS[0:n, :], PS[0:n, 4, 0:256]).then_inc(s_Be, 1)
                else:
                    dve.tensor_copy(KVWIN[:, j - 1, :], PS[:, 4, 0:256]).then_inc(s_Be, 1)
                dve.wait_ge(s_tg, j + 1)
                gat = GATS[0:n, :] if j == 0 else GAT[:, j - 1, :]
                dve.tensor_scalar(gat, gat, 1.0, 0.25, ALU.add, ALU.mult).then_inc(s_gate, 1)
            dve_keys(dve, 8)
            for j in IDX:
                n = rows(j)
                zb = ZNS[0:n, :] if j == 0 else Z[:, j - 1, :]
                sl = SLD[j % 2]
                dve.wait_ge(s_rs2, j + 1)
                if j >= 2:
                    dve.wait_ge(s_oD[j % 2], 16 * (j // 2))
                    dve.wait_ge(s_dT, j - 1)
                    if True:
                        dve.wait_ge(s_vs, 9 + j - 1)
                if j == 0:
                    dve.wait_ge(s_oW, 16 * 9)
                    dve.wait_ge(s_cos, 16)
                    dve.wait_ge(s_kT, 9)
                dve.tensor_scalar(sl[0:n, 0:256], PS[0:n, 3, 0:256], RSTD2[0:n, j, 0:1], None, ALU.mult)\
                    .then_inc(s_cqn, 1)
                dve.scalar_tensor_tensor(sl[0:n, 256:384], PS[0:n, 3, 256:384], RSTD2[0:n, j, 1:2],
                                         GKV[0:n, :], ALU.mult, ALU.mult).then_inc(s_ckv, 1)
                cos, sin = (cosS, sinS) if j == 0 else (COSSIN[:, 0, j - 1, :], COSSIN[:, 1, j - 1, :])
                kr = PS[0:n, 3, 384:448]
                dve.tensor_tensor(RT[0][0:n, 0:64], kr, cos[0:n, :], ALU.mult).then_inc(s_r1, 1)
                dve.tensor_tensor(RT[1][0:n, 0:32], kr[:, 32:64], sin[0:n, 0:32], ALU.mult).then_inc(s_r1, 1)
                dve.tensor_tensor(RT[1][0:n, 32:64], kr[:, 0:32], sin[0:n, 32:64], ALU.mult).then_inc(s_r1, 1)
                dve.wait_ge(s_r1, 3 * j + 3)
                dve.wait_ge(s_ckv, j + 1)
                dve.tensor_tensor(sl[0:n, 384:448], RT[0][0:n, 0:64], RT[1][0:n, 0:64], ALU.add).then_inc(s_kr, 1)
                dve.wait_ge(s_tC, j + 1)
                dve.scalar_tensor_tensor(zb[:, 0:512], zb[:, 0:512], 1.0, PS[0:n, 2, :], ALU.add, ALU.mult)\
                    .then_inc(s_zC, 1)
                dve.wait_ge(s_tE, j + 1)
                dve.scalar_tensor_tensor(zb[:, 512:1024], zb[:, 512:1024], 1.0, PS[0:n, 4, :], ALU.add, ALU.mult)\
                    .then_inc(s_zE, 1)
                dve_latents(dve, j)

        def dve_keys(dve, j):
            n = rows(j)
            dve.wait_ge(s_kT, j + 1)
            if j == 1:
                dve.wait_ge(s_gdma, 16)
            ks, kw = (KSELTS, KWINTS) if j == 0 else (KSELT[:, tok(j)], KWINT[:, tok(j)])
            dve.tensor_copy(ks, PS[:, 5, 0:n]).then_inc(s_kTe, 1)
            dve.tensor_copy(kw, PS[:, 5, 128:128 + n]).then_inc(s_kTe, 1)

        def dve_latents(dve, j):
            n = rows(j)
            dve.wait_ge(s_dT, j + 1)
            cq, ck, kr = (CQTS[:, :, :], CKVTS, KRTS) if j == 0 else (CQT[:, :, tok(j)], CKVT[:, tok(j)], KRT[:, tok(j)])
            dve.tensor_tensor(cq, PS[:, 5, 0:256].rearrange("p (k t) -> p k t", k=2)[:, :, 0:n],
                              GQT.rearrange("p (k t) -> p k t", t=1).to_broadcast([P, 2, n]), ALU.mult)\
                .then_inc(s_dTe, 1)
            dve.tensor_copy(ck, PS[:, 5, 256:256 + n]).then_inc(s_dTe, 1)
            dve.tensor_copy(kr[0:64, :], PS[0:64, 6, 0:n]).then_inc(s_dTe, 1)

        def pool_projection(pool):
            pool.memset(RBA[32:33, :], 1.0).then_inc(s_ones, 1)
            pool.memset(ONE9[0:1, :], 1.0).then_inc(s_ones, 1)
            pool.wait_ge(s_ones, 2)
            pool.wait_ge(s_cst, 16 * 7)
            pool.memset(SSQ[:, 0:1], 0.0).then_inc(s_ms, 1)
            for j in IDX:
                n = rows(j)
                pool.wait_ge(s_ssq, j + 1)
                pool.tensor_scalar(RSTD[0:n, j:j + 1], SSQ[0:n, j:j + 1], 1.0 / DM, EPS, ALU.mult, ALU.add)\
                    .then_inc(s_ms, 1)
                pool.wait_ge(s_ms, j + 2)
                pool.tensor_tensor(RSTD[0:n, j:j + 1], RSTD[0:n, j:j + 1], mhalf[0:n, :], ALU.pow)\
                    .then_inc(s_rstd, 1)
                pool.wait_ge(s_Ae, j + 1)
                if j == 0:
                    pool.memset(SSQ2[:, 0, :], 0.0).then_inc(s_vs, 1)
                else:
                    if j == 1:
                        pool.wait_ge(s_udma, 16)
                    pool.tensor_copy(VSEL[:, j - 1, :], SLA[j % 2][:, 384:512]).then_inc(s_vs, 1)
            for j in IDX:
                n = rows(j)
                pool.wait_ge(s_sq2, j + 1)
                for c, m in ((0, 256), (1, 128)):
                    pool.tensor_scalar(RSTD2[0:n, j, c:c + 1], SSQ2[0:n, j, c:c + 1], 1.0 / m, EPS,
                                       ALU.mult, ALU.add).then_inc(s_ms2, 1)
                pool.wait_ge(s_ms2, 2 * j + 2)
                pool.tensor_tensor(RSTD2[0:n, j, :], RSTD2[0:n, j, :], mhalf[0:n, :].to_broadcast([n, 2]),
                                   ALU.pow).then_inc(s_rs2, 1)
                pool.wait_ge(s_ckv, j + 1)
                if j == 0:
                    pool.memset(CCON[:, :], 0.0).then_inc(s_vs, 1)
                else:
                    pool.tensor_copy(CKV[:, j - 1, :], SLD[j % 2][:, 256:384]).then_inc(s_vs, 1)

        s_wu, s_kcv, s_tt = sem("s_wu"), sem("s_kcv"), sem("s_tt")
        s_kcp = sem("s_kcp")
        s_wt, s_X, s_wl, s_fl, s_kv, s_ql = sem("s_wt"), sem("s_X"), sem("s_wl"), sem("s_fl"), sem("s_kv"), sem("s_ql")
        s_rdA, s_rdD = sem("s_rdA"), sem("s_rdD")
        WT_AT, X_AT, WL_AT, FL_AT, KV_AT, QL_AT = 0, 2, 4, 5, 7, 8
        s_con, s_conv, s_cmp, s_cmpv = sem("s_con"), sem("s_conv"), sem("s_cmp"), sem("s_cmpv")
        s_qr, s_qr1, s_qr2, s_qrT, s_qrA = sem("s_qr"), sem("s_qr1"), sem("s_qr2"), sem("s_qrT"), sem("s_qrA")
        PSF = PS[:, :, :].rearrange("p b c -> p (b c)")

        def sp_prep(sp):
            sp.wait_ge(s_E, 9)
            sp.wait_ge(s_dT, 9)
            sp.dma_start(WUQ[:, :, :, :].rearrange("p k h e -> p k (h e)"),
                         w_uq[0].rearrange("(k p) h e -> p k (h e)", p=P)).then_inc(s_wu, 16)
            sp.dma_start(WUK[:, :, :].rearrange("p h n -> p (h n)"), w_uk[0].rearrange("r h n -> r (h n)"))\
                .then_inc(s_wu, 16)
            sp.dma_start(WUV[:, :, :].rearrange("p h n -> p (h n)"), w_uv[0].rearrange("r h n -> r (h n)"))\
                .then_inc(s_wu, 16)
            sp.wait_ge(s_oA[0], 80)
            sp.wait_ge(s_oA[1], 64)
            sp.dma_start(KCVP[0:NCH_P, :, :],
                         nsa_p[0, 0].rearrange("(n l) c g d -> n l (c g d)", l=16)[:, :, 0:256]).then_inc(s_kcv, 16)
            sp.wait_ge(s_udma, 16)
            sp.dma_start(TT[:, :, :], bass.AP(U_dram.tensor, 0, [[1, P], [383, H], [1, 256]])).then_inc(s_tt, 16)

        def pe_prep(pe):
            pe.wait_ge(s_wu, 48)
            pe.wait_ge(s_zTe, 1)
            pe.wait_ge(s_zE, 9)
            pe.wait_ge(s_zC, 9)
            pe.wait_ge(s_dTe, 27)
            for h in range(HB):
                pe.transpose(PS[:, h, 0:128], WUQ[:, 0, h, 0:128], ident)
                pe.transpose(PS[:, h, 128:256], WUQ[:, 1, h, 0:128], ident)
                pe.transpose(PS[:, h, 256:384], WUK[:, h, :], ident).then_inc(s_wt, 1)
            for c in range(2):
                for lp in range(8):
                    if lp == 0:
                        pe.wait_ge(s_kcp, 2 * c + 2)
                    for g in range(G):
                        q = (lp * 2 + g) * 64
                        mm = pe.transpose(PS[:, 4 + 2 * c + q // 512, q % 512:q % 512 + 64],
                                          KCPP[0:64, 2 * c + g, 2 * lp:2 * lp + 2, :].rearrange("p l d -> p (l d)"),
                                          ident[0:64, 0:64])
                    if lp in (3, 7):
                        mm.then_inc(s_X, 1)
            pe.wait_ge(s_rdA, WT_AT + 2)
            pe.wait_ge(s_rdD, WT_AT + 2)
            for k in range(2):
                for h in range(HB):
                    mm = pe.matmul(PS[:, k, P * h:P * h + P], WT[:, h, P * k:P * k + P], WT[:, h, 256:384],
                                   start=True, stop=True)
                mm.then_inc(s_wl, 1)
            pe.wait_ge(s_cc, 16 * 8)
            for c in range(2):
                for lp in range(8):
                    mm = pe.matmul(PS[:, 2, 2 * c:2 * c + 2], WC[:, c, lp, :], PET[:, c, lp, :],
                                   start=(lp == 0), stop=(lp == 7))
            mm.then_inc(s_con, 1)
            pe.wait_ge(s_rdA, X_AT + 2)
            pe.wait_ge(s_rdD, X_AT + 2)
            for c in range(2):
                for lp in range(8):
                    mm = pe.matmul(PS[:, 3, P * c:P * c + P], WC[:, c, lp, :], XTP[:, c, lp, :],
                                   start=(lp == 0), stop=(lp == 7))
            mm.then_inc(s_cmp, 1)
            pe.wait_ge(s_tt, 16)
            for m in range(4):
                pe.matmul(PS[:, 4 + m, :], flip, TT[:, 2 * m:2 * m + 2, :], start=True, stop=True).then_inc(s_fl, 1)
            pe.wait_ge(s_rdA, WL_AT + 1)
            pe.wait_ge(s_rdD, WL_AT + 1)
            pe.wait_ge(s_cmpv, 2)
            for g in range(G):
                for s in range(2):
                    mm = pe.matmul(PS[64 * g:64 * g + 64, 0, 0:NCMP_P], ident[:, 64 * s:64 * s + 64],
                                   RBP[:, 0, 64 * g + s:64 * g + s + NCMP_P], start=(s == 0), stop=(s == 1))
            mm.then_inc(s_kv, 1)
            for g in range(G):
                for s in range(2):
                    mm = pe.matmul(PS[0:NCMP_P, 1, 64 * g:64 * g + 64], RBP[:, 1, 64 * g + s:64 * g + s + NCMP_P],
                                   ident[:, 64 * s:64 * s + 64], start=(s == 0), stop=(s == 1))
            mm.then_inc(s_kv, 1)
            pe.wait_ge(s_rdA, FL_AT + 2)
            pe.wait_ge(s_rdD, FL_AT + 2)
            pe.wait_ge(s_conv, 2)
            for m in range(9):
                bank = 2 + m % 6
                if m >= 6:
                    pe.wait_ge(s_rdA, QL_AT + ((m - 6) // 2 + 1 if m % 2 == 0 else (m - 5) // 2))
                    pe.wait_ge(s_rdD, QL_AT + ((m - 5) // 2 if m % 2 == 1 else max((m - 6) // 2, 1)))
                for h in ((m // 2,) if m < 8 else range(HB)):
                    for k in range(2):
                        out = PS[:, bank, :] if m < 8 else PS[:, bank, RS * h:RS * h + RS]
                        rhs = CQT[:, k, 512 * (m % 2):512 * (m % 2) + 512] if m < 8 else CQTS[:, k, :]
                        mm = pe.matmul(out, WLAT[:, k, h, :], rhs, start=(k == 0), stop=(k == 1))
                mm.then_inc(s_ql, 1)
            pe.wait_ge(s_rdA, KV_AT + 1)
            pe.wait_ge(s_rdD, KV_AT + 1)
            pe.wait_ge(s_rdA, QL_AT + 5)
            pe.wait_ge(s_rdD, QL_AT + 4)
            for i in range(10):
                if i < 9:
                    n = P if i < 8 else RS
                    if i >= 2:
                        pe.wait_ge(s_qr1, 3 * (i - 1))
                    for k in range(2):
                        lhs = CQT[:, k, P * i:P * i + P] if i < 8 else CQTS[:, k, :]
                        mm = pe.matmul(PS[0:n, i % 2, 0:256], lhs, WUQ[:, k, :, 128:192], start=(k == 0), stop=(k == 1))
                    mm.then_inc(s_qr, 1)
                if i >= 1:
                    n = P if i < 9 else RS
                    pe.wait_ge(s_qr2, i)
                    if i >= 3:
                        pe.wait_ge(s_qrA, i - 2)
                    for h in range(HB):
                        mm = pe.transpose(PS[0:64, 2 + (i - 1) % 2, P * h:P * h + n],
                                          QRN[(i - 1) % 2][0:n, 64 * h:64 * h + 64], ident[0:n, 0:n])
                    mm.then_inc(s_qrT, 1)

        def act_prep(act):
            for h in (0, 2):
                act.wait_ge(s_wt, h + 1)
                act.activation(WT[:, h, :], PS[:, h, 0:384], ACT.Copy).then_inc(s_rdA, 1)
            for c in range(2):
                act.wait_ge(s_X, 2 * c + 1)
                act.activation(XTP[:, c, 0:4, :].rearrange("p l n -> p (l n)"), PS[:, 4 + 2 * c, :], ACT.Copy)\
                    .then_inc(s_rdA, 1)
            act.wait_ge(s_wl, 1)
            act.activation(WLAT[:, 0, :, :].rearrange("p h r -> p (h r)"), PS[:, 0, :], ACT.Copy).then_inc(s_rdA, 1)
            for m in (0, 2):
                act.wait_ge(s_fl, m + 1)
                act.activation(BT[:, 2 * m:2 * m + 2, :].rearrange("p h c -> p (h c)"), PS[:, 4 + m, :], ACT.Copy)\
                    .then_inc(s_rdA, 1)
            act.wait_ge(s_kv, 1)
            act.activation(KCTP, PS[:, 0, 0:NCMP_P], ACT.Copy).then_inc(s_rdA, 1)
            for m in (0, 2, 4, 6, 8):
                act.wait_ge(s_ql, m + 1)
                if m < 8:
                    act.activation(QLATT[:, m // 2, 0:512], PS[:, 2 + m % 6, :], ACT.Copy).then_inc(s_rdA, 1)
                else:
                    act.activation(QLTS[:, :, :].rearrange("p h t -> p (h t)"), PS[:, 4, 0:128], ACT.Copy)\
                        .then_inc(s_rdA, 1)
            for i in range(9):
                act.wait_ge(s_qrT, i + 1)
                src = PS[0:64, 2 + i % 2, :].rearrange("p (h t) -> p h t", h=HB)
                if i < 8:
                    act.activation(QRT[0:64, :, P * i:P * i + P], src, ACT.Copy).then_inc(s_qrA, 1)
                else:
                    act.activation(QRTS[0:64, :, :], src[:, :, 0:RS], ACT.Copy).then_inc(s_qrA, 1)

        def dve_prep(dve):
            for h in (1, 3):
                dve.wait_ge(s_wt, h + 1)
                dve.tensor_copy(WT[:, h, :], PS[:, h, 0:384]).then_inc(s_rdD, 1)
            for c in range(2):
                dve.wait_ge(s_X, 2 * c + 2)
                dve.tensor_copy(XTP[:, c, 4:8, :].rearrange("p l n -> p (l n)"), PS[:, 5 + 2 * c, :]).then_inc(s_rdD, 1)
            dve.wait_ge(s_wl, 2)
            dve.tensor_copy(WLAT[:, 1, :, :].rearrange("p h r -> p (h r)"), PS[:, 1, :]).then_inc(s_rdD, 1)
            dve.wait_ge(s_con, 1)
            dve.wait_ge(s_vs, 18)
            cb = PS[:, 2, 0:4].rearrange("p (c s) -> p c s", c=2)
            for s in range(2):
                dve.tensor_copy(CCON[64 * s:64 * s + 64, :], cb[64 * s:64 * s + 64, :, s]).then_inc(s_conv, 1)
            dve.wait_ge(s_conv, 2)
            dve.wait_ge(s_cmp, 1)
            for c in range(2):
                dve.tensor_scalar(RBP[:, c, :], PS[:, 3, P * c:P * c + P], CCON[:, c:c + 1], None, ALU.add)\
                    .then_inc(s_cmpv, 1)
            for m in (1, 3):
                dve.wait_ge(s_fl, m + 1)
                dve.tensor_copy(BT[:, 2 * m:2 * m + 2, :].rearrange("p h c -> p (h c)"), PS[:, 4 + m, :])\
                    .then_inc(s_rdD, 1)
            dve.wait_ge(s_kv, 2)
            dve.tensor_copy(VCP[0:NCMP_P, :], PS[0:NCMP_P, 1, 0:128]).then_inc(s_rdD, 1)
            for m in (1, 3, 5, 7):
                dve.wait_ge(s_ql, m + 1)
                dve.tensor_copy(QLATT[:, m // 2, 512:1024], PS[:, 2 + m % 6, :]).then_inc(s_rdD, 1)
            for i in range(9):
                n = P if i < 8 else RS
                dve.wait_ge(s_qr, i + 1)
                if i >= 2:
                    dve.wait_ge(s_qrT, i - 1)
                cos, sin = (COSSIN[:, 0, i, :], COSSIN[:, 1, i, :]) if i < 8 else (cosS, sinS)

                def heads(ap, w):
                    return ap[0:n, :].rearrange("p (h e) -> p h e", h=1).to_broadcast([n, HB, w])

                src = PS[0:n, i % 2, 0:256].rearrange("p (h e) -> p h e", h=HB)
                qn, qm = (b[i % 2][0:n, :].rearrange("p (h e) -> p h e", h=HB) for b in (QRN, QRM))
                dve.tensor_tensor(qn, src, heads(cos, 64), ALU.mult).then_inc(s_qr1, 1)
                dve.tensor_tensor(qm[:, :, 0:32], src[:, :, 32:64], heads(sin[:, 0:32], 32), ALU.mult).then_inc(s_qr1, 1)
                dve.tensor_tensor(qm[:, :, 32:64], src[:, :, 0:32], heads(sin[:, 32:64], 32), ALU.mult)\
                    .then_inc(s_qr1, 1)
                dve.wait_ge(s_qr1, 3 * i + 3)
                dve.tensor_tensor(qn, qn, qm, ALU.add).then_inc(s_qr2, 1)

        def pool_prep(pool):
            pool.wait_ge(s_kcv, 16)
            for c in range(4):
                pool.tensor_copy(KCPP[0:64, c, :, :], KCVP[0:64, :, 64 * c:64 * c + 64]).then_inc(s_kcp, 1)

        UNITS = []
        for i in range(NT):
            both = [(0, 1)] if i < 4 else [(0,), (1,)]
            for kind in ("sel", "win"):
                k0 = max(0, i - 4) if kind == "win" else 0
                UNITS += [(kind, i, gs, k0, (i + 1 - k0) * P) for gs in both]
            UNITS.append(("cmp", i, (0, 1), 0, min(NCMP_P, 8 * i + 7)))
            UNITS.append(("mla", i, (0,), 0, (i + 1) * P))
        N = len(UNITS)
        assert N % 2 == 0
        CHUNKS, CH_OF = [], []
        for u, (kind, i, gs, k0, nk) in enumerate(UNITS):
            tiles = len(gs) * (1 if kind == "cmp" else nk // P)
            CH_OF.append([])
            for t0 in range(0, tiles, 4):
                CH_OF[u].append(len(CHUNKS))
                CHUNKS.append((u, t0, min(4, tiles - t0)))
        NCH = len(CHUNKS)
        EVA = (NCH + 1) // 2
        EVD = NCH // 2
        EXTRA = [u for u in range(N) if UNITS[u][0] in ("mla", "cmp")]
        s_stage, s_qk, s_bias, s_mx, s_neg, s_exp = (sem(f"s_at_{n}") for n in
                                                     ("stage", "qk", "bias", "mx", "neg", "exp"))
        s_trc, s_evA, s_evD, s_av, s_acc = (sem(f"s_at_{n}") for n in ("trc", "evA", "evD", "av", "acc"))
        s_olt, s_yb, s_su, s_rc, s_cf, s_ya = (sem(f"s_at_{n}") for n in ("olt", "yb", "su", "rc", "cf", "ya"))

        s_alone = sem("s_alone")

        def settle(eng):
            eng.sem_inc(s_alone, 1)

        def scores(k, lo, hi, gs):
            base = 1024 * (k % 2)
            if len(gs) == 2:
                return PSF[:, base:base + 1024].rearrange("p (g c) -> p g c", g=2)[:, :, lo:hi]
            return PSF[:, base + lo:base + hi].rearrange("p (g c) -> p g c", g=1)

        def pe_attention(pe):
            pe.wait_ge(s_qrA, 9)
            pe.sem_inc(s_qk, 1)
            pe.sem_inc(s_trc, NCH)
            pe.sem_inc(s_av, 2)
            pe.sem_inc(s_yb, 2)
            with pe.Fori(0, R) as r:
                pe.wait_ge(s_stage, 4 * r + 8)
                for step in range(N + 4):
                    if step < N:
                        u = step
                        kind, i, gs, k0, nk = UNITS[u]
                        pe.wait_ge(s_exp, r * N + u + 1)
                        q = slice(P * i, P * i + P)
                        for gi, g in enumerate(gs):
                            base = 1024 * (u % 2) + 512 * gi
                            for lo in range(0, nk, 512):
                                hi = min(nk, lo + 512)
                                out = PSF[:, base + lo:base + hi]
                                if kind == "mla":
                                    pe.matmul(out, QLH[:, q], CKVT[:, lo:hi], start=True, stop=False)
                                    mm = pe.matmul(out, QRH[:, q], KRT[:, lo:hi], start=False, stop=True)
                                else:
                                    keys = {"sel": KSELT, "win": KWINT, "cmp": KCTP}[kind]
                                    mm = pe.matmul(out, QSH[g][:, q], keys[:, P * k0 + lo:P * k0 + hi],
                                                   start=True, stop=True)
                        mm.then_inc(s_qk, 1)
                    if step >= 4:
                        u = step - 4
                        pe.wait_ge(s_olt, r * N + u + 1)
                        out = PS[:, 6 + u % 2, 256:384]
                        if UNITS[u][0] == "mla":
                            mm = pe.matmul(out, OTB[u % 2], WUV[:, bass.ds(r, 1), :], start=True, stop=True)
                        else:
                            mm = pe.transpose(out, OTB[u % 2], ident)
                        mm.then_inc(s_yb, 1)
                    if 3 <= step < N + 3:
                        u = step - 3
                        kind, i, gs, k0, nk = UNITS[u]
                        last = CH_OF[u][-1]
                        pe.wait_ge(s_evA, r * EVA + (last + 2) // 2 + 2)
                        if last >= 1:
                            pe.wait_ge(s_evD, r * EVD + (last + 1) // 2 + 2)
                        pe.wait_ge(s_acc, r * N + u + 1)
                        ob = PS[:, 6 + u % 2, :]
                        tiles = PTB[u % 2]
                        if kind == "mla":
                            for kb in range(i + 1):
                                mm = pe.matmul(ob[:, 0:128], CKV[:, kb, :], tiles[:, kb, :],
                                               start=(kb == 0), stop=(kb == i))
                        else:
                            nb = 1 if kind == "cmp" else nk // P
                            kk = nk if kind == "cmp" else P
                            if 32 < kk < P:
                                settle(pe)
                            for kb in range(nb):
                                for gi, g in enumerate(gs):
                                    v = {"sel": lambda: VSEL[:, kb, 64 * g:64 * g + 64],
                                         "win": lambda: KVWIN[:, k0 + kb, 128 + 64 * g:192 + 64 * g],
                                         "cmp": lambda: VCP[0:nk, 64 * g:64 * g + 64]}[kind]()
                                    mm = pe.matmul(ob[64 * g:64 * g + 64, 0:128], v, tiles[0:kk, gi * nb + kb, :],
                                                   start=(kb == 0), stop=(kb == nb - 1))
                        mm.then_inc(s_av, 1)
                    if 2 <= step < N + 2:
                        u = step - 2
                        kind, i, gs, k0, nk = UNITS[u]
                        pe.wait_ge(s_exp, r * N + u + 3)
                        for c in CH_OF[u]:
                            _, t0, nt = CHUNKS[c]
                            if c % 2 == 0:
                                pe.wait_ge(s_evA, r * EVA + c // 2 + 2)
                            else:
                                pe.wait_ge(s_evD, r * EVD + c // 2 + 2)
                            for t in range(t0, t0 + nt):
                                if kind == "cmp":
                                    src, kk = PB[u % 2][:, 512 * t:512 * t + P], P
                                else:
                                    nb = nk // P
                                    o = 512 * (t // nb) + P * (t % nb) if len(gs) == 2 else P * t
                                    src, kk = PB[u % 2][:, o:o + P], P
                                mm = pe.transpose(PS[0:kk, 4 + c % 2, P * (t - t0):P * (t - t0) + P], src, ident)
                            mm.then_inc(s_trc, 1)

        def act_attention(act):
            act.sem_inc(s_exp, 2)
            act.sem_inc(s_evA, 2)
            with act.Fori(0, R) as r:
                for step in range(N + 3):
                    if 2 <= step < N + 2:
                        act_evac(act, r, step - 2)
                    if 3 <= step:
                        u = step - 3
                        gs = (0, 1) if UNITS[u][0] == "mla" else UNITS[u][2]
                        rg = slice(64 * gs[0], 64 * gs[-1] + 64)
                        act.wait_ge(s_av, r * N + u + 3)
                        act.wait_ge(s_yb, r * N + u + 1)
                        act.activation(OTB[u % 2][rg, :], PS[rg, 6 + u % 2, 0:128], ACT.Copy).then_inc(s_olt, 1)
                    if step < N:
                        u = step
                        kind, i, gs, k0, nk = UNITS[u]
                        act.wait_ge(s_neg, r * N + u + 1)
                        c_free = CH_OF[u - 2][-1] + 1 if u >= 2 else CH_OF[u - 2][-1] + 1 - NCH
                        act.wait_ge(s_trc, r * NCH + c_free + NCH)
                        for gi, g in enumerate(gs):
                            ins = act.activation(PB[u % 2][:, 512 * gi:512 * gi + nk], scores(u, 0, nk, gs)[:, gi, :],
                                                 ACT.Exp, bias=NM[:, u % 2, gi:gi + 1],
                                                 scale=MSC if kind == "mla" else 1.0,
                                                 accum_out=SU[:, u % 8, gi:gi + 1])
                        ins.then_inc(s_exp, 1)

        def evac(eng, r, u, mine, copy, done):
            kind, i, gs, k0, nk = UNITS[u]
            for c in CH_OF[u]:
                if c % 2 != mine:
                    continue
                _, t0, nt = CHUNKS[c]
                kk = nk if kind == "cmp" else P
                eng.wait_ge(s_trc, r * NCH + c + 1 + NCH)
                eng.wait_ge(s_av, r * N + u + 1)
                copy(PTB[u % 2][0:kk, t0:t0 + nt, :],
                     PS[0:kk, 4 + c % 2, 0:P * nt].rearrange("p (t q) -> p t q", t=nt)).then_inc(done, 1)

        def act_evac(act, r, u):
            evac(act, r, u, 0, lambda o, i: act.activation(o, i, ACT.Copy), s_evA)

        def dve_attention(dve):
            dve.wait_ge(s_qrA, 9)
            dve.sem_inc(s_evD, 2)
            dve.sem_inc(s_acc, 2)
            with dve.Fori(0, R) as r:
                for step in range(N + 4):
                    if step < N:
                        u = step
                        kind, i, gs, k0, nk = UNITS[u]
                        dve.wait_ge(s_qk, r * N + u + 2)
                        btr = BT[:, :, :].rearrange("p (g r) c -> p r g c", g=G)[:, bass.ds(r, 1)]\
                            .rearrange("p o g c -> p (o g) c")
                        bcr = BC[:, :, :].rearrange("p n (g r) -> p r g n", g=G)[:, bass.ds(r, 1)]\
                            .rearrange("p o g n -> p (o g) n")
                        gl = slice(gs[0], gs[-1] + 1)
                        if kind in ("sel", "win"):
                            if kind == "win" and i >= 4:
                                s = scores(u, 0, P, gs)
                                dve.tensor_tensor(s, s, wmask.rearrange("p (o c) -> p o c", o=1), ALU.add)
                            near = min(256, nk)
                            s = scores(u, nk - near, nk, gs)
                            ins = dve.tensor_tensor(s, s, btr[:, gl, 256 - near:256], ALU.add)
                        elif kind == "cmp":
                            lo = max(0, 8 * i - 8)
                            s = scores(u, lo, nk, gs)
                            ins = dve.tensor_tensor(s, s, bcr[:, :, lo - 8 * i + 8:nk - 8 * i + 8], ALU.add)
                        else:
                            s = scores(u, nk - P, nk, gs)
                            ins = dve.tensor_tensor(s, s, cmask.rearrange("p (o c) -> p o c", o=1), ALU.add)
                        ins.then_inc(s_bias, 1)
                        dve.wait_ge(s_bias, r * N + u + 1)
                        nm = NM[:, u % 2, 0:len(gs)]
                        ins = dve.tensor_reduce(nm, scores(u, 0, nk, gs), AX, ALU.max, negate=True)
                        if u in EXTRA:
                            ins.then_inc(s_mx, 1)
                            dve.wait_ge(s_mx, r * len(EXTRA) + EXTRA.index(u) + 1)
                            if kind == "cmp":
                                ins = dve.tensor_scalar(nm, nm, 1e29, None, ALU.min)
                            else:
                                ins = dve.tensor_scalar(nm, nm, MSC, None, ALU.mult)
                        ins.then_inc(s_neg, 1)
                    if 2 <= step < N + 2:
                        evac(dve, r, step - 2, 1, dve.tensor_copy, s_evD)
                    if 4 <= step:
                        dve_finish(dve, r, step - 4)

        def dve_finish(dve, r, u):
            kind, i, gs, k0, nk = UNITS[u]
            n = len(gs)
            su = SU[:, u % 8, 0:n]
            dve.wait_ge(s_exp, r * N + u + 3)
            if kind == "cmp":
                dve.tensor_scalar(su, su, 1e-30, None, ALU.max).then_inc(s_su, 1)
                dve.wait_ge(s_su, r * NT + i + 1)
            dve.reciprocal(RC[:, 0:n], su).then_inc(s_rc, 1)
            dve.wait_ge(s_rc, r * N + u + 1)
            if kind == "mla":
                dve.tensor_scalar(CF[:, 0:1], RC[:, 0:1], 0.5, None, ALU.mult).then_inc(s_cf, 1)
            else:
                br = ("cmp", "sel", "win").index(kind)
                gt = GAT[:, i, :].rearrange("p (g r b) -> p r g b", g=G, r=R)[:, bass.ds(r, 1), gs[0]:gs[-1] + 1, br]
                dve.tensor_tensor(CF[:, 0:n].rearrange("p (o g) -> p o g", o=1),
                                  RC[:, 0:n].rearrange("p (o g) -> p o g", o=1), gt, ALU.mult).then_inc(s_cf, 1)
            dve.wait_ge(s_cf, r * N + u + 1)
            ob = PS[:, 6 + u % 2, :]
            if kind == "mla":
                dve.wait_ge(s_yb, r * N + u + 3)
                zi = Z[:, i, 512:1024].rearrange("p (h v) -> p h v", h=HB)[:, bass.ds(r, 1), :]
                dve.scalar_tensor_tensor(zi, ob[:, 256:384].rearrange("p (h v) -> p h v", h=1), CF[:, 0:1], zi,
                                         ALU.mult, ALU.mult).then_inc(s_acc, 1)
                return
            dve.wait_ge(s_yb, r * N + u + 3)
            dve.wait_ge(s_acc, r * N + u + 2)
            for gi, g in enumerate(gs):
                o = ob[:, 256 + 64 * g:320 + 64 * g]
                if kind == "sel":
                    ins = dve.tensor_scalar(YACC[:, i, g, :], o, CF[:, gi:gi + 1], None, ALU.mult)
                else:
                    ins = dve.scalar_tensor_tensor(YACC[:, i, g, :], o, CF[:, gi:gi + 1], YACC[:, i, g, :],
                                                   ALU.mult, ALU.add)
            if kind == "cmp":
                ins.then_inc(s_ya, 1)
                dve.wait_ge(s_ya, r * NT + i + 1)
                zi = Z[:, i, 0:512].rearrange("p (r c) -> p r c", r=R)[:, bass.ds(r, 1), :]
                ins = dve.tensor_tensor(zi, zi, YACC[:, i, :, :].rearrange("p g d -> p (g d)")
                                        .rearrange("p (o c) -> p o c", o=1), ALU.mult)
            ins.then_inc(s_acc, 1)

        def pool_attention(pool):
            pool.wait_ge(s_qrA, 9)
            pool.wait_ge(s_rdA, QL_AT + 5)
            pool.wait_ge(s_rdD, QL_AT + 4)
            for rows_ in (QSH[0][64:128, :], QRH[64:128, :], KRT[64:128, :], QSH[1][0:64, :]):
                pool.memset(rows_, 0.0).then_inc(s_stage, 1)
            pool.wait_ge(s_stage, 4)
            with pool.Fori(0, R) as r:
                pool.wait_ge(s_qk, r * N + 1)
                for g in range(G):
                    rg = slice(64 * g, 64 * g + 64)
                    pool.tensor_copy(QSH[g][rg, :], QT[rg, bass.ds(r, 1), :].rearrange("p o t -> p (o t)"))\
                        .then_inc(s_stage, 1)
                pool.wait_ge(s_stage, 4 * r + 6)
                pool.tensor_copy(QLH, QLATT[:, bass.ds(r, 1), :].rearrange("p o t -> p (o t)")).then_inc(s_stage, 1)
                pool.wait_ge(s_stage, 4 * r + 7)
                pool.tensor_copy(QRH[0:64, :], QRT[0:64, bass.ds(r, 1), :].rearrange("p o t -> p (o t)"))\
                    .then_inc(s_stage, 1)
                pool.wait_ge(s_stage, 4 * r + 8)
        WOUT = view(33280, 8192).rearrange("p (k n) -> p k n", k=8)
        XO = [view(22912 + 1024 * n, 1024) for n in range(2)]
        GP, GF = view(24960, 1024), view(25984, 1024)
        YTO = [view(27008 + 1024 * n, 1024).rearrange("p (k t) -> p k t", k=8) for n in range(2)]
        YO = [view(29056 + 1024 * n, 1024) for n in range(2)]
        GPS = view(31104, 1024)
        JK = view(32128, 1024)
        SSO, RSO = small(9), small(9)
        s_wo, s_gp, s_xo, s_yT, s_yTA, s_yTD = sem("s_wo"), sem("s_gp"), sems("s_xo", 2), sem("s_yT"), sem("s_yTA"), sem("s_yTD")
        s_po, s_g1, s_g2, s_so, s_mo, s_ro, s_yo = (sem(f"s_out_{n}") for n in
                                                           ("mm", "gate", "res", "ssq", "ms", "rstd", "y"))
        s_out = sems("s_out_st", 2)
        y_t = [y_sample.rearrange("b t d -> (b t) d")] + [y_prompt[0, P * i:P * i + P, :] for i in range(NT)]

        def sp_out_loads(sp):
            sp.wait_ge(s_acc, R * N + 2)
            for g in range(G):
                sp.dma_start(WOUT[64 * g:64 * g + 64, 0:4, :],
                             w_out[0, 256 * g:256 * g + 256, :].rearrange("(r d) n -> d r n", r=R)).then_inc(s_wo, 16)
            sp.dma_start(WOUT[:, 4:8, :], w_out[0, 512:1024, :].rearrange("(h v) n -> v h n", h=HB)).then_inc(s_wo, 16)
            sp.dma_start(GP, gate_dram[8:9, :].to_broadcast([P, DM])).then_inc(s_gp, 16)
            sp.dma_start(GF, g_final.rearrange("(o n) -> o n", o=1).to_broadcast([P, DM])).then_inc(s_gp, 16)
            for b in range(NB):
                sp.dma_start(GPS[4 * b:4 * b + 4, :], gate_dram[b:b + 1, :].to_broadcast([TS, DM])).then_inc(s_gp, 16)

        def sp_out(sp, tiles, at):
            for m, j in enumerate(tiles, at):
                if m >= 2:
                    sp.wait_ge(s_g2, 2 * (m - 1))
                sp.dma_start(XO[m % 2][0:rows(j), :], x_t[j]).then_inc(s_xo[m % 2], 16)
                if m > at:
                    sp.wait_ge(s_yo, m)
                    sp.dma_start(y_t[tiles[m - 1 - at]], YO[(m - 1) % 2][0:rows(tiles[m - 1 - at]), :])\
                        .then_inc(s_out[(m - 1) % 2], 16)
            m = at + len(tiles)
            sp.wait_ge(s_yo, m)
            sp.dma_start(y_t[tiles[-1]], YO[(m - 1) % 2][0:rows(tiles[-1]), :]).then_inc(s_out[(m - 1) % 2], 16)

        def pe_out(pe, tiles, at):
            def transposes(m, j):
                if m >= 1:
                    pe.wait_ge(s_yTA, m)
                    pe.wait_ge(s_yTD, m)
                for f in range(8):
                    mm = pe.transpose(PS[:, f // 4, P * (f % 4):P * (f % 4) + P], Z[:, j - 1, P * f:P * f + P], ident)
                mm.then_inc(s_yT, 1)

            if tiles[0] >= 1:
                transposes(at, tiles[0])
            for m, j in enumerate(tiles, at):
                n = rows(j)
                if m + 1 < at + len(tiles):
                    transposes(m + 1, tiles[m + 1 - at])
                if m == 0:
                    pe.wait_ge(s_wo, 48)
                pe.wait_ge(s_yTA, m + 1)
                pe.wait_ge(s_yTD, m + 1)
                if m >= 2:
                    pe.wait_ge(s_g1, 2 * (m - 1))
                for c in range(2):
                    for f in range(8):
                        mm = pe.matmul(PS[0:n, 2 + 2 * (m % 2) + c, :], YTO[m % 2][:, f, 0:n],
                                       WOUT[:, f, 512 * c:512 * c + 512], start=(f == 0), stop=(f == 7))
                    mm.then_inc(s_po, 1)

        def out_copies(eng, copy, bank, done, m):
            if m >= 2:
                eng.wait_ge(s_po, 2 * (m - 1))
            eng.wait_ge(s_yT, m + 1)
            copy(YTO[m % 2][:, 4 * bank:4 * bank + 4, :], PS[:, bank, :].rearrange("p (k t) -> p k t", k=4))\
                .then_inc(done, 1)

        def act_out(act, tiles, at):
            copy = lambda o, i: act.activation(o, i, ACT.Copy)
            for m, j in enumerate(tiles, at):
                n = rows(j)
                if m == at and j >= 1:
                    out_copies(act, copy, 0, s_yTA, m)
                if m + 1 < at + len(tiles):
                    out_copies(act, copy, 0, s_yTA, m + 1)
                act.wait_ge(s_g2, 2 * m + 2)
                if m >= 1:
                    act.wait_ge(s_so, m)
                act.activation(JK[0:n, :], YO[m % 2][0:n, :], ACT.Square, accum_out=SSO[0:n, m:m + 1]).then_inc(s_so, 1)

        def dve_out(dve, tiles, at):
            for m, j in enumerate(tiles, at):
                n = rows(j)
                if m == at and j >= 1:
                    out_copies(dve, dve.tensor_copy, 1, s_yTD, m)
                if m + 1 < at + len(tiles):
                    out_copies(dve, dve.tensor_copy, 1, s_yTD, m + 1)
                if m == 0:
                    dve.wait_ge(s_gp, 160)
                dve.wait_ge(s_xo[m % 2], 16 * (m // 2 + 1))
                if m >= 2:
                    dve.wait_ge(s_out[m % 2], 16 * (m // 2))
                gate = GPS if j == 0 else GP
                for c in range(2):
                    cs = slice(512 * c, 512 * c + 512)
                    dve.wait_ge(s_po, 2 * m + c + 1)
                    dve.tensor_tensor(YO[m % 2][0:n, cs], PS[0:n, 2 + 2 * (m % 2) + c, :], gate[0:n, cs], ALU.mult)\
                        .then_inc(s_g1, 1)
                    dve.wait_ge(s_g1, 2 * m + c + 1)
                    dve.tensor_tensor(YO[m % 2][0:n, cs], YO[m % 2][0:n, cs], XO[m % 2][0:n, cs], ALU.add)\
                        .then_inc(s_g2, 1)
                dve.wait_ge(s_ro, m + 1)
                dve.scalar_tensor_tensor(YO[m % 2][0:n, :], YO[m % 2][0:n, :], RSO[0:n, m:m + 1], GF[0:n, :],
                                         ALU.mult, ALU.mult).then_inc(s_yo, 1)

        def pool_out(pool, tiles, at):
            for m, j in enumerate(tiles, at):
                n = rows(j)
                pool.wait_ge(s_so, m + 1)
                pool.tensor_scalar(RSO[0:n, m:m + 1], SSO[0:n, m:m + 1], 1.0 / DM, EPS, ALU.mult, ALU.add)\
                    .then_inc(s_mo, 1)
                pool.wait_ge(s_mo, m + 1)
                pool.tensor_tensor(RSO[0:n, m:m + 1], RSO[0:n, m:m + 1], mhalf[0:n, :], ALU.pow).then_inc(s_ro, 1)

        KCPD = view(0, 4096).rearrange("p (c l d) -> p c l d", c=4, l=16)
        XTD = view(4096, 4096).rearrange("p (c l n) -> p c l n", c=2, l=8)
        GT1 = view(4096, 900)
        GT2 = view(5120, 900)
        KSV = view(8192, 4096).rearrange("p (i c) -> p i c", i=NPG)
        MLD = view(12288, 3072).rearrange("p (i c) -> p i c", i=NPG)
        WND = view(15360, 1024).rearrange("p (j c) -> p j c", j=4)
        KCVD = view(16384, 4096).rearrange("p (l c) -> p l c", l=16)
        KTD = view(20480, 2048)
        CKTD = view(22528, 2048)
        KWTD = view(24576, 512)
        RBD = view(25088, 512).rearrange("p (c n) -> p c n", c=2)
        KCTD, VCD, PCD = view(25600, 128), view(25728, 128), view(25856, 128)
        KRTD = view(27008, 2048)
        PSD = view(29056, 512).rearrange("p (i q) -> p i q", i=NPG)
        PMD = view(29568, 256).rearrange("p (i q) -> p i q", i=NPG)
        PWD = view(29824, 128).rearrange("p (j q) -> p j q", j=4)
        dcur = [29952]

        def dsm(n):
            dcur[0] += n
            assert dcur[0] <= 31104
            return view(dcur[0] - n, n)

        QBD, QLB, QRB = dsm(32), dsm(16), dsm(16)
        KND = dsm(16).rearrange("p (k t) -> p k t", k=4)
        MK = dsm(33)
        IM, RK, IMS, IML, PCT = dsm(30), dsm(30), dsm(8), dsm(32), dsm(32)
        PWN, PMN, PSN = dsm(32), dsm(16), dsm(32)
        NMD, SUD, RCD = dsm(4), dsm(4), dsm(4)
        OY, OM = dsm(128), dsm(128)
        NBS, NCB = small(132), small(8)
        OLTS = dsm(128).rearrange("p (h t) -> p h t", h=HB)
        YTS = dsm(128).rearrange("p (r t) -> p r t", r=R)
        SSD, SMD, SWD = view(41984, 2052), view(44036, 2052), view(46088, 516)
        VND = view(46604, 384)
        L = PAST

        ITEMS = ["Rk", "Rv", "kcT", "cmp", "vc", "imp", "m0", "m1", "m2", "m3", "mn", "w", "wn",
                 "s0", "s1", "s2", "s3", "sn"]
        NI = len(ITEMS)
        BY_ACT = ["Rv", "kcT", "vc", "m0", "m1", "m2", "m3"]
        NIA, NID = len(BY_ACT), NI - len(BY_ACT)
        NC = 28
        PCT_C, KR_C, WK_C, PM_C, PW_C, PS_C, PSN_C, OM_C, FOLD_C = 16, 17, 21, 22, 23, 24, 25, 26, 27
        DSTEPS = 16

        s_nb, s_kc, s_ks, s_ml, s_wn, s_vn, s_ws = (sem(f"s_d_{n}") for n in ("nb", "kc", "ks", "ml", "wn", "vn", "ws"))
        s_kp, s_qb, s_tp, s_eA, s_eD, s_I, s_iA, s_iD = (sem(f"s_d_{n}") for n in
                                                        ("kp", "qb", "tp", "eA", "eD", "I", "iA", "iD"))
        s_pc, s_impl, s_nmx, s_ex, s_avs, s_avm, s_avw, s_dv = (sem(f"s_d_{n}") for n in
                                                                ("pc", "impl", "nmx", "ex", "avs", "avm", "avw", "dv"))
        s_oy, s_om, s_mk, s_yb2, s_ob = (sem(f"s_d_{n}") for n in ("oy", "om", "mk", "yb", "ob"))

        def items_before(name, by_act):
            return sum((x in BY_ACT) == by_act for x in ITEMS[:ITEMS.index(name) + 1])

        def wait_item(eng, b, name):
            if name in BY_ACT:
                eng.wait_ge(s_iA, b * NIA + items_before(name, True) + 1)
            else:
                eng.wait_ge(s_iD, b * NID + items_before(name, False) + 1)

        def wait_chunk(eng, b, c):
            eng.wait_ge(s_eA if c % 2 == 0 else s_eD, b * (NC // 2) + c // 2 + 3)

        def load_sequence(sp, b):
            pages = []
            for n in range(NPG):
                pg = sp.value_load(PT_SB[0:1, bass.ds(b * NPG + n, 1)], min_val=0, max_val=NPHYS - 1)
                pages.append(pg)
                if n == 0:
                    sp.wait_ge(s_kp, 4 * b + 4)
                sp.dma_start(KCVD[8 * n:8 * n + 8, :, :],
                             cache_nsa[0, bass.ds(pg, 1)].rearrange("o (n l) c g d -> (o n) l (c g d)", l=16)[:, :, 0:256])\
                    .then_inc(s_kc, 16)
            sp.wait_ge(s_avw, b + 1)
            if not isinstance(b, int):
                settle(sp)
                sp.wait_ge(s_ws, 32 * b)
            sp.dma_start(WND[:, :, :].rearrange("p j c -> p (j c)"),
                         state_win[0, bass.ds(b, 1)].rearrange("o (p j) c g d -> (o p) (j c g d)", j=4)).then_inc(s_wn, 16)
            sp.wait_ge(s_avs, b + 1)
            for n, pg in enumerate(pages):
                sp.dma_start(KSV[:, n, :],
                             cache_nsa[0, bass.ds(pg, 1)].rearrange("o t c g d -> (o t) (c g d)")[:, 256:512])\
                    .then_inc(s_ks, 16)
            sp.wait_ge(s_avm, b + 1)
            for n, pg in enumerate(pages):
                sp.dma_start(MLD[:, n, :], cache_mla[0, bass.ds(pg, 1)].rearrange("o t c -> (o t) c"))\
                    .then_inc(s_ml, 16)
            sp.dma_start(VND[0:TS, 0:128],
                         nsa_s[0, bass.ds(b, 1), :, 3].rearrange("o t g d -> (o t) (g d)")).then_inc(s_vn, 16)
            sp.dma_start(VND[0:TS, 128:256],
                         win_s[0, bass.ds(b, 1), 508:512, 1].rearrange("o t g d -> (o t) (g d)")).then_inc(s_vn, 16)
            sp.dma_start(VND[0:TS, 256:384], mla_s[0, bass.ds(b, 1), :, 0:128].rearrange("o t c -> (o t) c"))\
                .then_inc(s_vn, 16)
            sp.wait_ge(s_wn, 16 * b + 16)
            for p0, n in ((1, 112), (113, 15)):
                sp.dma_start(win_s[0, bass.ds(b, 1), 4 * (p0 - 1):4 * (p0 - 1 + n)]
                             .rearrange("o (p j) c g d -> (o p) (j c g d)", j=4),
                             WND[p0:p0 + n, :, :].rearrange("p j c -> p (j c)")).then_inc(s_ws, 16)

        def sp_decode_first(sp):
            sp.wait_ge(s_udma, 16)
            sp.wait_ge(s_oA[0], 80)
            sp.wait_ge(s_oW, 16 * 9)
            sp.wait_ge(s_oD[0], 80)
            for t in range(TS):
                sp.dma_start(NBS[t:RS:TS, :], U_dram[:, 127 - t:259 - t]).then_inc(s_nb, 16)
                sp.dma_start(NCB[t:RS:TS, :], U_dram[:, 142 - t:142 - t + 113:16], allow_slow_non_contiguous=True)\
                    .then_inc(s_nb, 16)
            load_sequence(sp, 0)

        def sp_decode(sp):
            with sp.Fori(1, NB) as b:
                load_sequence(sp, b)

        def pe_decode(pe):
            for s, n in ((s_tp, NC + 1), (s_avs, 1), (s_avm, 1), (s_avw, 1), (s_I, 1)):
                pe.sem_inc(s, n)

        def pe_decode_loop(pe):
            pe.wait_ge(s_g1, 16)
            pe.wait_ge(s_nb, 128)

            def chunk(b, c):
                wait_chunk(pe, b, c - 4) if c >= 4 else pe.wait_ge(
                    s_eA if c % 2 == 0 else s_eD, b * (NC // 2) + c // 2 + 1)
                bank = PS[:, c % 4, :]
                if c < 8:
                    k, lp0 = c // 4, 2 * (c % 4)
                    if c in (0, 4):
                        pe.wait_ge(s_kp, 4 * b + 2 * k + 6)
                    for n in range(4):
                        lp, g = lp0 + n // 2, n % 2
                        mm = pe.transpose(bank[:, P * n:P * n + P],
                                          KCPD[:, 2 * k + g, 2 * lp:2 * lp + 2, :].rearrange("p l d -> p (l d)"), ident)
                elif c < 12:
                    if c == 8:
                        pe.wait_ge(s_ks, b * 256 + 256)
                    for n in range(4):
                        mm = pe.transpose(bank[:, P * n:P * n + P], KSV[:, 4 * (c - 8) + n, 0:128], ident)
                elif c < 16:
                    if c == 12:
                        pe.wait_ge(s_ml, b * 256 + 256)
                    for n in range(4):
                        mm = pe.transpose(bank[:, P * n:P * n + P], MLD[:, 4 * (c - 12) + n, 0:128], ident)
                elif c == PCT_C:
                    pe.wait_ge(s_pc, b + 1)
                    settle(pe)
                    mm = pe.transpose(bank[:, 0:RS], PCD[0:RS, :], ident[0:RS, 0:RS])
                elif c < WK_C:
                    settle(pe)
                    for n in range(4):
                        mm = pe.transpose(bank[0:64, P * n:P * n + P], MLD[:, 4 * (c - KR_C) + n, 128:192], ident)
                elif c == WK_C:
                    pe.wait_ge(s_wn, 16 * b + 16)
                    for j in range(4):
                        mm = pe.transpose(bank[:, P * j:P * j + P], WND[:, j, 0:128], ident)
                elif c == PW_C:
                    pe.wait_ge(s_ex, 4 * b + 3)
                    settle(pe)
                    for j in range(4):
                        pe.transpose(bank[:, RS * j:RS * j + RS], SWD[0:RS, j:509 + j:4], ident[0:RS, 0:RS])
                    mm = pe.transpose(bank[0:TS, 128:128 + RS], SWD[0:RS, 512:516], ident[0:RS, 0:RS])
                elif c == PM_C:
                    pe.wait_ge(s_ex, 4 * b + 2)
                    settle(pe)
                    for n in range(NPG):
                        pe.transpose(bank[:, 16 * n:16 * n + 16], SMD[0:16, P * n:P * n + P], ident[0:16, 0:16])
                    mm = pe.transpose(bank[0:TS, 256:272], SMD[0:16, L:L + TS], ident[0:16, 0:16])
                elif c == PS_C:
                    pe.wait_ge(s_ex, 4 * b + 4)
                    settle(pe)
                    for n in range(NPG):
                        mm = pe.transpose(bank[:, RS * n:RS * n + RS], SSD[0:RS, P * n:P * n + P], ident[0:RS, 0:RS])
                elif c == PSN_C:
                    settle(pe)
                    mm = pe.transpose(bank[0:TS, 0:RS], SSD[0:RS, L:L + TS], ident[0:RS, 0:RS])
                elif c == OM_C:
                    pe.wait_ge(s_om, b + 1)
                    settle(pe)
                    mm = pe.transpose(bank[:, 0:16], OM[0:16, :], ident[0:16, 0:16])
                else:
                    pe.wait_ge(s_oy, b + 1)
                    mm = pe.matmul(bank[:, 0:16], OY[0:RS, :], foldm, start=True, stop=True)
                mm.then_inc(s_tp, 1)

            def item(b, name):
                m = ITEMS.index(name)
                if m >= 3:
                    wait_item(pe, b, ITEMS[m - 3])
                else:
                    pe.wait_ge(s_iD, b * NID + 1)
                    pe.wait_ge(s_iA, b * NIA + 1)
                bank = PS[:, 4 + m % 3, :]
                if name in ("Rk", "Rv"):
                    k = int(name == "Rv")
                    wait_chunk(pe, b, 4 * k + 2)
                    wait_chunk(pe, b, 4 * k + 3)
                    for lp in range(8):
                        mm = pe.matmul(bank[:, 0:256], WC[:, k, lp, :], XTD[:, k, lp, :], start=(lp == 0), stop=(lp == 7))
                elif name == "kcT":
                    wait_item(pe, b, "Rk")
                    for g in range(G):
                        for s in range(2):
                            mm = pe.matmul(bank[64 * g:64 * g + 64, 0:NCMP_S], ident[:, 64 * s:64 * s + 64],
                                           RBD[:, 0, P * g + s:P * g + s + NCMP_S], start=(s == 0), stop=(s == 1))
                elif name == "vc":
                    wait_item(pe, b, "Rv")
                    for g in range(G):
                        for s in range(2):
                            mm = pe.matmul(bank[0:NCMP_S, 64 * g:64 * g + 64],
                                           RBD[:, 1, P * g + s:P * g + s + NCMP_S], ident[:, 64 * s:64 * s + 64],
                                           start=(s == 0), stop=(s == 1))
                elif name == "cmp":
                    wait_item(pe, b, "kcT")
                    pe.wait_ge(s_qb, 8 * b + 12)
                    mm = pe.matmul(bank[0:RS, 0:NCMP_S], QBD, KCTD[:, 0:NCMP_S], start=True, stop=True)
                elif name == "imp":
                    pe.wait_ge(s_impl, b + 1)
                    mm = pe.matmul(bank[0:RS, 0:NSB], IML[0:NCMP_S, :], CC[:, :], start=True, stop=True)
                elif name in ("m0", "m1", "m2", "m3"):
                    q = int(name[1])
                    wait_chunk(pe, b, 12 + q)
                    wait_chunk(pe, b, KR_C + q)
                    pe.matmul(bank[0:16, :], QLB, CKTD[:, 512 * q:512 * q + 512], start=True, stop=False)
                    mm = pe.matmul(bank[0:16, :], QRB, KRTD[:, 512 * q:512 * q + 512], start=False, stop=True)
                elif name == "mn":
                    pe.matmul(bank[0:16, 0:TS], QLB, KND[:, 2, :], start=True, stop=False)
                    mm = pe.matmul(bank[0:16, 0:TS], QRB, KND[:, 3, :], start=False, stop=True)
                elif name == "w":
                    wait_chunk(pe, b, WK_C)
                    mm = pe.matmul(bank[0:RS, :], QBD, KWTD, start=True, stop=True)
                elif name == "wn":
                    mm = pe.matmul(bank[0:RS, 0:TS], QBD, KND[:, 1, :], start=True, stop=True)
                elif name == "sn":
                    mm = pe.matmul(bank[0:RS, 0:TS], QBD, KND[:, 0, :], start=True, stop=True)
                else:
                    q = int(name[1])
                    wait_chunk(pe, b, 8 + q)
                    mm = pe.matmul(bank[0:RS, :], QBD, KTD[:, 512 * q:512 * q + 512], start=True, stop=True)
                mm.then_inc(s_I, 1)

            OB = PS[:, 7, :]
            with pe.Fori(0, NB) as b:
                for c in range(4):
                    chunk(b, c)
                item(b, "Rk")
                for c in range(4, 8):
                    chunk(b, c)
                item(b, "Rv")
                for c in range(8, 12):
                    chunk(b, c)
                for name in ("kcT", "cmp", "vc"):
                    item(b, name)
                for c in range(12, 21):
                    chunk(b, c)
                item(b, "imp")
                chunk(b, WK_C)
                for name in ITEMS[6:]:
                    item(b, name)
                chunk(b, PM_C)
                pe.wait_ge(s_ob, b + 1)
                wait_item(pe, b, "vc")
                wait_chunk(pe, b, PCT_C)
                pe.matmul(OB[0:RS, 0:128], PCT[0:NCMP_S, :], VCD[0:NCMP_S, :], start=True, stop=True)
                wait_chunk(pe, b, PM_C)
                pe.wait_ge(s_vn, 48 * b + 48)
                for n in range(NPG):
                    pe.matmul(OB[0:16, 384:512], PMD[:, n, :], MLD[:, n, 0:128], start=(n == 0), stop=False)
                pe.matmul(OB[0:16, 384:512], PMN[0:TS, :], VND[0:TS, 256:384], start=False, stop=True).then_inc(s_avm, 1)
                chunk(b, PW_C)
                wait_chunk(pe, b, PW_C)
                for j in range(4):
                    pe.matmul(OB[0:RS, 128:256], PWD[:, j, :], WND[:, j, 128:256], start=(j == 0), stop=False)
                pe.matmul(OB[0:RS, 128:256], PWN[0:TS, :], VND[0:TS, 128:256], start=False, stop=True).then_inc(s_avw, 1)
                chunk(b, PS_C)
                chunk(b, PSN_C)
                wait_chunk(pe, b, PS_C)
                wait_chunk(pe, b, PSN_C)
                for n in range(NPG):
                    pe.matmul(OB[0:RS, 256:384], PSD[:, n, :], KSV[:, n, 128:256], start=(n == 0), stop=False)
                pe.matmul(OB[0:RS, 256:384], PSN[0:TS, :], VND[0:TS, 0:128], start=False, stop=True).then_inc(s_avs, 1)
                chunk(b, OM_C)
                chunk(b, FOLD_C)
            wait_chunk(pe, NB - 1, OM_C)
            wait_chunk(pe, NB - 1, FOLD_C)
            for h in range(HB):
                mm = pe.matmul(PS[:, 0, RS * h:RS * h + RS], WUV[:, h, :], OLTS[:, h, :], start=True, stop=True)
            mm.then_inc(s_yb2, 1)

        def read_chunk(eng, copy, b, c):
            eng.wait_ge(s_tp, b * NC + c + 2 + NC)
            bank = PS[:, c % 4, :]
            done = s_eA if c % 2 == 0 else s_eD
            if c < 8:
                ins = copy(XTD[:, c // 4, 2 * (c % 4):2 * (c % 4) + 2, :].rearrange("p l n -> p (l n)"), bank)
            elif c < 12:
                ins = copy(KTD[:, 512 * (c - 8):512 * (c - 7)], bank)
            elif c < 16:
                ins = copy(CKTD[:, 512 * (c - 12):512 * (c - 11)], bank)
            elif c == PCT_C:
                ins = copy(PCT, bank[:, 0:RS])
            elif c < WK_C:
                ins = copy(KRTD[0:64, 512 * (c - KR_C):512 * (c - KR_C + 1)], bank[0:64, :])
            elif c == WK_C:
                ins = copy(KWTD.rearrange("p (k j) -> p j k", j=4), bank.rearrange("p (j k) -> p j k", j=4))
            elif c == PW_C:
                copy(PWD[:, :, :].rearrange("p j q -> p (j q)"), bank[:, 0:128])
                ins = copy(PWN[0:TS, :], bank[0:TS, 128:128 + RS])
            elif c == PM_C:
                copy(PMD[:, :, :].rearrange("p j q -> p (j q)"), bank[:, 0:256])
                ins = copy(PMN[0:TS, :], bank[0:TS, 256:272])
            elif c == PS_C:
                ins = copy(PSD[:, :, :].rearrange("p j q -> p (j q)"), bank)
            elif c == PSN_C:
                ins = copy(PSN[0:TS, :], bank[0:TS, 0:RS])
            elif c == OM_C:
                ins = copy(OLTS[:, :, bass.ds(4 * b, TS)], bank[:, 0:16].rearrange("p (h t) -> p h t", h=HB))
            else:
                ins = copy(YTS[:, :, bass.ds(4 * b, TS)], bank[:, 0:16].rearrange("p (r t) -> p r t", r=R))
            ins.then_inc(done, 1)

        def item_bank(eng, b, name):
            m = ITEMS.index(name)
            eng.wait_ge(s_I, b * NI + m + 2)
            return PS[:, 4 + m % 3, :]

        def act_decode(act):
            act.sem_inc(s_eA, 2)
            act.sem_inc(s_iA, 1)
            copy = lambda o, i: act.activation(o, i, ACT.Copy)
            ev = lambda b, *cs: [read_chunk(act, copy, b, c) for c in cs]

            def expo(b, n, buf, rows_, cols):
                act.wait_ge(s_nmx, 4 * b + n + 1)
                act.activation(buf[0:rows_, 0:cols], buf[0:rows_, 0:cols], ACT.Exp, bias=NMD[0:rows_, n:n + 1],
                               accum_out=SUD[0:rows_, n:n + 1]).then_inc(s_ex, 1)

            with act.Fori(0, NB) as b:
                ev(b, 0, 2, 4, 6)
                bank = item_bank(act, b, "Rv")
                act.activation(RBD[:, 1, :], bank[:, 0:256], ACT.Identity, bias=CCON[:, 1:2]).then_inc(s_iA, 1)
                ev(b, 8, 10)
                bank = item_bank(act, b, "kcT")
                copy(KCTD[:, 0:NCMP_S], bank[:, 0:NCMP_S]).then_inc(s_iA, 1)
                expo(b, 0, PCD, RS, NCMP_S)
                bank = item_bank(act, b, "vc")
                copy(VCD[0:NCMP_S, :], bank[0:NCMP_S, 0:128]).then_inc(s_iA, 1)
                ev(b, 12, 14, 16, 18, 20)
                for q in range(4):
                    bank = item_bank(act, b, f"m{q}")
                    act.activation(SMD[0:16, 512 * q:512 * q + 512], bank[0:16, :], ACT.Copy, scale=MSC).then_inc(s_iA, 1)
                expo(b, 1, SMD, 16, L + TS)
                ev(b, 22)
                expo(b, 2, SWD, RS, 516)
                expo(b, 3, SSD, RS, L + TS)
                ev(b, 24, 26)

        def dve_decode(dve):
            dve.sem_inc(s_eD, 2)
            dve.sem_inc(s_iD, 1)
            dve.sem_inc(s_ob, 1)
            for k in range(2):
                dve.wait_ge(s_out[k], 64)
            dve.memset(MK[0:RS, :], 0.0).then_inc(s_mk, 1)
            dve.memset(PCD[0:RS, :], 0.0).then_inc(s_mk, 1)
            dve.wait_ge(s_mk, 2)
            dve.wait_ge(s_nb, 128)
            ev = lambda b, *cs: [read_chunk(dve, dve.tensor_copy, b, c) for c in cs]
            with dve.Fori(0, NB) as b:
                count = [0]

                def step(ins):
                    count[0] += 1
                    ins.then_inc(s_dv, 1)
                    dve.wait_ge(s_dv, b * DSTEPS + count[0])

                def wait_dve_items(name):
                    dve.wait_ge(s_iD, b * NID + items_before(name, False) + 1)

                ev(b, 1, 3)
                bank = item_bank(dve, b, "Rk")
                dve.tensor_scalar(RBD[:, 0, :], bank[:, 0:256], CCON[:, 0:1], None, ALU.add).then_inc(s_iD, 1)
                ev(b, 5, 7, 9, 11)
                bank = item_bank(dve, b, "cmp")
                dve.tensor_copy(PCD[0:RS, 0:NCMP_S], bank[0:RS, 0:NCMP_S]).then_inc(s_iD, 1)
                wait_dve_items("cmp")
                near = PCD[0:RS, NCMP_S - 8:NCMP_S]
                step(dve.tensor_tensor(near, near, NCB[0:RS, :], ALU.add))
                dve.tensor_reduce(NMD[0:RS, 0:1], PCD[0:RS, 0:NCMP_S], AX, ALU.max, negate=True).then_inc(s_nmx, 1)
                ev(b, 13)
                dve.wait_ge(s_ex, 4 * b + 1)
                step(dve.reciprocal(RCD[0:RS, 0:1], SUD[0:RS, 0:1]))
                dve.tensor_scalar(PCD[0:RS, 0:NCMP_S], PCD[0:RS, 0:NCMP_S], RCD[0:RS, 0:1], None, ALU.mult)\
                    .then_inc(s_pc, 1)
                ev(b, 15)
                wait_chunk(dve, b, PCT_C)
                step(dve.tensor_reduce(IMS[0:NCMP_S, :].rearrange("p (g t) -> p g t", g=G),
                                       PCT[0:NCMP_S, :].rearrange("p (g r t) -> p g t r", g=G, r=R), AX, ALU.add))
                dve.tensor_copy(IML[0:NCMP_S, :].rearrange("p (g r t) -> p g r t", g=G, r=R),
                                IMS[0:NCMP_S, :].rearrange("p (g r t) -> p g r t", g=G, r=1)
                                .to_broadcast([NCMP_S, G, R, TS])).then_inc(s_impl, 1)
                ev(b, 17, 19)
                bank = item_bank(dve, b, "imp")
                dve.tensor_copy(IM[0:RS, :], bank[0:RS, 1:31]).then_inc(s_iD, 1)
                wait_dve_items("imp")
                sq = [RS, NFREE, NFREE]
                imi = IM[0:RS, :].rearrange("p (o i) -> p o i", o=1).to_broadcast(sq)
                imj = IM[0:RS, :].rearrange("p (j o) -> p j o", o=1).to_broadcast(sq)
                g1 = GT1[0:RS, :].rearrange("p (j i) -> p j i", j=NFREE)
                g2 = GT2[0:RS, :].rearrange("p (j i) -> p j i", j=NFREE)
                dve.tensor_tensor(g1, imi, imj, ALU.is_gt)
                step(dve.tensor_tensor(g2, imi, imj, ALU.is_equal))
                step(dve.tensor_tensor(GT2[0:RS, :], GT2[0:RS, :], lowS, ALU.mult))
                step(dve.tensor_tensor(GT1[0:RS, :], GT1[0:RS, :], GT2[0:RS, :], ALU.add))
                step(dve.tensor_reduce(RK[0:RS, :], g1, AX, ALU.add))
                step(dve.tensor_scalar(MK[0:RS, 1:31], RK[0:RS, :], float(KEEP) - 0.5, BIG, ALU.is_ge, ALU.mult))
                ev(b, 21)
                bank = item_bank(dve, b, "mn")
                dve.scalar_tensor_tensor(SMD[0:16, L:L + TS], bank[0:16, 0:TS], MSC, cmS[0:16, :], ALU.mult, ALU.add)\
                    .then_inc(s_iD, 1)
                wait_dve_items("mn")
                wait_item(dve, b, "m3")
                dve.tensor_reduce(NMD[0:16, 1:2], SMD[0:16, 0:L + TS], AX, ALU.max, negate=True).then_inc(s_nmx, 1)
                bank = item_bank(dve, b, "w")
                dve.tensor_copy(SWD[0:RS, 0:512], bank[0:RS, :]).then_inc(s_iD, 1)
                wait_dve_items("w")
                dve.tensor_tensor(SWD[0:RS, 0:TS], SWD[0:RS, 0:TS], wmS, ALU.add)
                step(dve.tensor_tensor(SWD[0:RS, 384:512], SWD[0:RS, 384:512], NBS[0:RS, 0:128], ALU.add))
                bank = item_bank(dve, b, "wn")
                dve.tensor_tensor(SWD[0:RS, 512:516], bank[0:RS, 0:TS], NBS[0:RS, 128:132], ALU.add).then_inc(s_iD, 1)
                wait_dve_items("wn")
                dve.tensor_reduce(NMD[0:RS, 2:3], SWD[0:RS, :], AX, ALU.max, negate=True).then_inc(s_nmx, 1)
                for q in range(4):
                    bank = item_bank(dve, b, f"s{q}")
                    dve.tensor_tensor(SSD[0:RS, 512 * q:512 * q + 512].rearrange("p (j c) -> p j c", j=8),
                                      bank[0:RS, :].rearrange("p (j c) -> p j c", j=8),
                                      MK[0:RS, 8 * q:8 * q + 8].rearrange("p (j o) -> p j o", o=1)
                                      .to_broadcast([RS, 8, 64]), ALU.add).then_inc(s_iD, 1)
                wait_dve_items("s3")
                step(dve.tensor_tensor(SSD[0:RS, L - 128:L], SSD[0:RS, L - 128:L], NBS[0:RS, 0:128], ALU.add))
                bank = item_bank(dve, b, "sn")
                dve.tensor_tensor(SSD[0:RS, L:L + TS], bank[0:RS, 0:TS], NBS[0:RS, 128:132], ALU.add).then_inc(s_iD, 1)
                wait_dve_items("sn")
                dve.tensor_reduce(NMD[0:RS, 3:4], SSD[0:RS, 0:L + TS], AX, ALU.max, negate=True).then_inc(s_nmx, 1)
                ev(b, 23, 25)
                dve.wait_ge(s_ex, 4 * b + 4)
                step(dve.reciprocal(RCD[0:RS, 2:4], SUD[0:RS, 2:4]))
                step(dve.reciprocal(RCD[0:16, 1:2], SUD[0:16, 1:2]))
                step(dve.tensor_scalar(RCD[0:16, 1:2], RCD[0:16, 1:2], 0.5, None, ALU.mult))
                gb = GBS[0:RS, bass.ds(b, 1), :].rearrange("p o c -> p (o c)")
                dve.tensor_tensor(RCD[0:RS, 2:3], RCD[0:RS, 2:3], gb[:, 2:3], ALU.mult)
                dve.tensor_tensor(RCD[0:RS, 3:4], RCD[0:RS, 3:4], gb[:, 1:2], ALU.mult)
                step(dve.tensor_copy(RCD[0:RS, 0:1], gb[:, 0:1]))
                dve.wait_ge(s_avm, b + 2)
                dve.wait_ge(s_avs, b + 2)
                ob = PS[:, 7, :]
                dve.tensor_scalar(OM[0:16, :], ob[0:16, 384:512], RCD[0:16, 1:2], None, ALU.mult).then_inc(s_om, 1)
                step(dve.tensor_scalar(OY[0:RS, :], ob[0:RS, 0:128], RCD[0:RS, 0:1], None, ALU.mult))
                step(dve.scalar_tensor_tensor(OY[0:RS, :], ob[0:RS, 128:256], RCD[0:RS, 2:3], OY[0:RS, :],
                                              ALU.mult, ALU.add))
                dve.scalar_tensor_tensor(OY[0:RS, :], ob[0:RS, 256:384], RCD[0:RS, 3:4], OY[0:RS, :],
                                         ALU.mult, ALU.add).then_inc(s_ob, 1)
                dve.wait_ge(s_ob, b + 2)
                dve.tensor_tensor(OY[0:RS, :], OY[0:RS, :], bdm, ALU.mult).then_inc(s_oy, 1)
                ev(b, 27)
                assert count[0] == DSTEPS, count[0]
            wait_chunk(dve, NB - 1, FOLD_C)
            dve.tensor_tensor(YTO[0][:, 0:4, 0:RS], YTS, ZTS[:, 0:4, :], ALU.mult).then_inc(s_yTA, 1)
            dve.wait_ge(s_yb2, 1)
            dve.tensor_tensor(YTO[0][:, 4:8, 0:RS], PS[:, 0, 0:128].rearrange("p (h t) -> p h t", h=HB),
                              ZTS[:, 4:8, :], ALU.mult).then_inc(s_yTD, 1)

        def pool_decode(pool):
            pool.wait_ge(s_yTA, NT)
            for k in range(2):
                pool.wait_ge(s_out[k], 64)
            for a in (KRTD[64:128, :], KND[64:128, 3, :], QRB[64:128, :]):
                pool.memset(a, 0.0).then_inc(s_qb, 1)
            pool.wait_ge(s_qb, 3)
            pool.memset(QBD, 0.0).then_inc(s_qb, 1)
            pool.wait_ge(s_qb, 4)
            with pool.Fori(0, NB) as b:
                pool.wait_ge(s_kc, b * 256 + 256)
                pool.wait_ge(s_tp, b * NC + 9)
                settle(pool)
                for c in range(4):
                    pool.tensor_copy(KCPD[:, c, :, :], KCVD[:, :, 64 * c:64 * c + 64]).then_inc(s_kp, 1)
                pool.wait_ge(s_I, b * NI + 1)
                pool.wait_ge(s_kp, 4 * b + 8)

                def lay_out(out, src):
                    pool.tensor_copy(out, src).then_inc(s_qb, 1)

                lay_out(QLB.rearrange("p (h t) -> p h t", h=HB), QLTS[:, :, bass.ds(4 * b, TS)])
                for k, keys in enumerate((KSELTS, KWINTS, CKVTS)):
                    lay_out(KND[:, k, :], keys[:, bass.ds(4 * b, TS)])
                pool.wait_ge(s_qb, 8 * b + 8)
                lay_out(KND[0:64, 3, :], KRTS[0:64, bass.ds(4 * b, TS)])
                lay_out(QRB[0:64, :].rearrange("p (h t) -> p h t", h=HB), QRTS[0:64, :, bass.ds(4 * b, TS)])
                for g in range(G):
                    lay_out(QBD[64 * g:64 * g + 64, 16 * g:16 * g + 16].rearrange("p (r t) -> p r t", r=R),
                            QTS[64 * g:64 * g + 64, :, bass.ds(4 * b, TS)])
                pool.wait_ge(s_qb, 8 * b + 12)
        PT_TILES = list(range(1, 9))
        block = ctx.enter_context(nc.Block())

        @block.sync
        def _(sp):
            sp_projection(sp)
            sp_prep(sp)
            sp_out_loads(sp)
            sp_decode_first(sp)
            sp_out(sp, PT_TILES, 0)
            sp_decode(sp)
            sp.wait_ge(s_yTD, NT + 1)
            sp_out(sp, [0], NT)
            sp.wait_ge(s_ws, 32 * NB)
            for s, n in ((s_oA[0], 80), (s_oA[1], 64), (s_oD[0], 80), (s_oD[1], 64), (s_oW, 144), (s_udma, 16),
                         (s_gdma, 16), (s_gsb, 128), (s_out[0], 80), (s_out[1], 64)):
                sp.wait_ge(s, n)

        @block.tensor
        def _(pe):
            pe_projection(pe)
            pe_prep(pe)
            pe_attention(pe)
            pe_decode(pe)
            pe_out(pe, PT_TILES, 0)
            pe_decode_loop(pe)
            pe_out(pe, [0], NT)

        @block.scalar
        def _(act):
            act_projection(act)
            act_prep(act)
            act_attention(act)
            act_out(act, PT_TILES, 0)
            act_decode(act)
            act_out(act, [0], NT)

        @block.vector
        def _(dve):
            dve_projection(dve)
            dve_prep(dve)
            dve_attention(dve)
            dve_out(dve, PT_TILES, 0)
            dve_decode(dve)
            dve_out(dve, [0], NT)

        @block.gpsimd
        def _(pool):
            pool_projection(pool)
            pool_prep(pool)
            pool_attention(pool)
            pool.sem_inc(s_kp, 4)
            pool_out(pool, PT_TILES, 0)
            pool_decode(pool)
            pool_out(pool, [0], NT)


_INS = ["x_prompt", "x_sample", "cache_nsa", "cache_mla", "state_win", "page_table", "c_prompt", "c_sample",
        "w_ada", "b_ada", "g_norm", "w_in", "w_cmp_k", "w_cmp_v", "pe_cmp_k", "pe_cmp_v", "rel_bias",
        "g_q_lat", "w_uq", "g_kv_lat", "w_uk", "w_uv", "w_out", "g_final"]
_OUTS = [(1, SEQ, DM), (NB, TS, DM), (1, 1, SEQ, 4, G, HD), (1, NB, TS, 4, G, HD), (1, 1, SEQ, 192),
         (1, NB, TS, 192), (1, 1, 512, 2, G, HD), (1, NB, 512, 2, G, HD)]


def kernel(**inputs):
    import concourse.bacc as bacc
    from concourse.bass_utils import run_bass_kernel_spmd as run

    nc = bacc.Bacc("TRN2", target_bir_lowering=False, num_devices=1)
    arrays, args = {}, []
    given = {n: np.ascontiguousarray(inputs[n]) for n in _INS}
    given.update(constants())
    for name, a in given.items():
        arrays[f"in_{name}"] = a
        args.append(nc.dram_tensor(f"in_{name}", a.shape, mybir.dt.from_np(a.dtype), kind="ExternalInput").ap())
    for i, shape in enumerate(_OUTS):
        args.append(nc.dram_tensor(f"out_{i}", shape, F32, kind="ExternalOutput").ap())
    build(nc, *args)
    r = run(nc, [arrays], core_ids=[0])
    return tuple(r.results[0][f"out_{i}"] for i in range(len(_OUTS)))
```
